# Optimizing a Trainium2 kernel written in Bass

```python
import jax, jax.numpy as jnp
from jax import lax
import numpy as np

D_MODEL = 1024
BATCH = 1
SEQ = 512
DEPTH = 1

CHUNK = 64
CONV_CH = 512
CONV_WIDTH = 31
HG_HEADS = 4
HG_DK = 128
HG_DV = 128
HG_WIDTH = HG_HEADS * HG_DK
SB_HEADS = 8
SB_DH = 64
SB_WIDTH = SB_HEADS * SB_DH
N_BRANCH = 3
D_FF = 4 * D_MODEL
QBLK = 128
EPS = 1e-6

IN_SIZES = (CONV_CH, CONV_CH, HG_WIDTH, HG_WIDTH, HG_HEADS * HG_DV, HG_HEADS * HG_DV,
            SB_WIDTH, SB_WIDTH, SB_WIDTH, N_BRANCH * D_MODEL)
D_IN = int(sum(IN_SIZES))
SPLIT_IDX = [int(v) for v in np.cumsum(IN_SIZES)[:-1]]


def rms_norm(x, g):
    xf = x.astype(jnp.float32)
    y = xf * lax.rsqrt(jnp.mean(xf * xf, axis=-1, keepdims=True) + EPS)
    return (y * g.astype(jnp.float32)).astype(x.dtype)

def layer_norm(x, g, b):
    xf = x.astype(jnp.float32)
    mu = jnp.mean(xf, axis=-1, keepdims=True)
    var = jnp.mean(jnp.square(xf - mu), axis=-1, keepdims=True)
    y = (xf - mu) * lax.rsqrt(var + EPS)
    return (y * g.astype(jnp.float32) + b.astype(jnp.float32)).astype(x.dtype)

def conv_branch(a, gate, w, b, ln_g, ln_b, w_proj):
    u = a * jax.nn.sigmoid(gate)
    u = lax.conv_general_dilated(
        u, w[:, None, :], window_strides=(1,), padding=((CONV_WIDTH - 1, 0),),
        dimension_numbers=('NWC', 'WIO', 'NWC'), feature_group_count=CONV_CH) + b
    u = jax.nn.silu(layer_norm(u, ln_g, ln_b))
    return u @ w_proj

def hgrn2_branch(q, f, i, g, lb, norm_g, w_proj):
    B, S, _ = q.shape
    n_chunks = S // CHUNK
    f32 = jnp.float32

    def heads(t, d):
        return t.reshape(B, n_chunks, CHUNK, HG_HEADS, d).transpose(1, 0, 3, 2, 4)

    k = (1.0 - lb.astype(f32)) * jax.nn.sigmoid(-f.astype(f32))
    log_f = jnp.log1p(-k)
    qh = heads(jax.nn.silu(q.astype(f32)), HG_DK)
    kh = heads(k, HG_DK)
    lfh = heads(log_f, HG_DK)
    vh = heads(i.astype(f32), HG_DV)
    causal = jnp.tril(jnp.ones((CHUNK, CHUNK), dtype=bool))[:, :, None]

    def step(state, inp):
        qc, kc, lc, vc = inp
        b = jnp.cumsum(lc, axis=2)
        o_inter = jnp.einsum('bhtk,bhkv->bhtv', qc * jnp.exp(b), state)
        rel = b[:, :, :, None, :] - b[:, :, None, :, :]
        decay = jnp.exp(jnp.where(causal, rel, -jnp.inf))
        scores = jnp.einsum('bhtsk,bhsk->bhts', qc[:, :, :, None, :] * decay, kc)
        o = o_inter + jnp.einsum('bhts,bhsv->bhtv', scores, vc)
        b_last = b[:, :, -1:, :]
        new_state = (jnp.exp(b_last[:, :, 0, :])[..., None] * state
                     + jnp.einsum('bhsk,bhsv->bhkv', kc * jnp.exp(b_last - b), vc))
        return new_state, o

    s0 = jnp.zeros((B, HG_HEADS, HG_DK, HG_DV), f32)
    _, o = lax.scan(step, s0, (qh, kh, lfh, vh))
    o = o.transpose(1, 0, 3, 2, 4).reshape(B, S, HG_HEADS, HG_DV)
    o = rms_norm(o, norm_g).reshape(B, S, HG_HEADS * HG_DV)
    o = (o * jax.nn.silu(g.astype(f32))).astype(q.dtype)
    return o @ w_proj

def stick_breaking_branch(q, k, v, qn_g, kn_g, w_proj):
    B, S, _ = q.shape
    qh = rms_norm(q.reshape(B, S, SB_HEADS, SB_DH), qn_g).transpose(0, 2, 1, 3)
    kh = rms_norm(k.reshape(B, S, SB_HEADS, SB_DH), kn_g).transpose(0, 2, 1, 3)
    vh = v.reshape(B, S, SB_HEADS, SB_DH).transpose(0, 2, 1, 3)
    scale = SB_DH ** -0.5
    outs = []
    for blk in range(S // QBLK):
        start, end = blk * QBLK, (blk + 1) * QBLK
        qb = qh[:, :, start:end]
        kb = kh[:, :, :end]
        vb = vh[:, :, :end]
        z = jnp.einsum('bhtd,bhsd->bhts', qb, kb).astype(jnp.float32) * scale
        t_pos = start + jnp.arange(QBLK)
        s_pos = jnp.arange(end)
        mask = s_pos[None, :] < t_pos[:, None]
        log_keep = jnp.where(mask, jax.nn.log_sigmoid(-z), 0.0)
        between = lax.cumsum(log_keep, axis=3, reverse=True) - log_keep
        a = jnp.where(mask, jnp.exp(jax.nn.log_sigmoid(z) + between), 0.0)
        outs.append(jnp.einsum('bhts,bhsd->bhtd', a.astype(vb.dtype), vb))
    o = jnp.concatenate(outs, axis=2).transpose(0, 2, 1, 3).reshape(B, S, SB_WIDTH)
    return o @ w_proj

def first_inputs(seed: int = 0) -> dict:
    key = jax.random.key(seed)
    ks = jax.random.split(key, 24)

    def nrm(k, shape, scale):
        return jax.random.normal(k, shape, jnp.float32) * scale

    L, D = DEPTH, D_MODEL
    return {
        "x": nrm(ks[0], (BATCH, SEQ, D), 1.0),
        "c": nrm(ks[1], (BATCH, D), 1.0),
        "mod_w": nrm(ks[2], (L, D, 6 * D), 0.5 * D ** -0.5),
        "mod_b": nrm(ks[3], (L, 6 * D), 0.01),
        "norm1_g": 1.0 + nrm(ks[4], (L, D), 0.02),
        "w_in": nrm(ks[5], (L, D, D_IN), D ** -0.5),
        "gate_b": nrm(ks[6], (L, N_BRANCH * D), 0.01),
        "conv_w": nrm(ks[7], (L, CONV_WIDTH, CONV_CH), CONV_WIDTH ** -0.5),
        "conv_b": nrm(ks[8], (L, CONV_CH), 0.01),
        "conv_ln_g": 1.0 + nrm(ks[9], (L, CONV_CH), 0.02),
        "conv_ln_b": nrm(ks[10], (L, CONV_CH), 0.01),
        "w_conv_proj": nrm(ks[11], (L, CONV_CH, D), CONV_CH ** -0.5),
        "hgrn_lb": nrm(ks[12], (L, HG_WIDTH), 0.5),
        "hgrn_norm_g": 1.0 + nrm(ks[13], (L, HG_DV), 0.02),
        "w_hgrn_proj": nrm(ks[14], (L, HG_HEADS * HG_DV, D), (HG_HEADS * HG_DV) ** -0.5),
        "sb_qn_g": 1.0 + nrm(ks[15], (L, SB_DH), 0.02),
        "sb_kn_g": 1.0 + nrm(ks[16], (L, SB_DH), 0.02),
        "w_sb_proj": nrm(ks[17], (L, SB_WIDTH, D), SB_WIDTH ** -0.5),
        "w_out": nrm(ks[18], (L, D, D), D ** -0.5),
        "norm2_g": 1.0 + nrm(ks[19], (L, D), 0.02),
        "mlp_w1": nrm(ks[20], (L, D, D_FF), D ** -0.5),
        "mlp_w2": nrm(ks[21], (L, D_FF, D), D_FF ** -0.5),
    }

def first_block(x, c, mod_w, mod_b, norm1_g, w_in, gate_b, conv_w, conv_b, conv_ln_g,
              conv_ln_b, w_conv_proj, hgrn_lb, hgrn_norm_g, w_hgrn_proj, sb_qn_g,
              sb_kn_g, w_sb_proj, w_out, norm2_g, mlp_w1, mlp_w2):
    B, S, D = x.shape
    p = jax.nn.softmax(hgrn_lb.astype(jnp.float32), axis=0)
    lower_bounds = jnp.cumsum(p, axis=0) - p[0:1]
    c_act = jax.nn.silu(c)
    for l in range(DEPTH):
        mod = c_act @ mod_w[l] + mod_b[l]
        sh1, sc1, g1, sh2, sc2, g2 = [m[:, None, :] for m in jnp.split(mod, 6, axis=-1)]

        h = rms_norm(x, norm1_g[l]) * (1.0 + sc1) + sh1
        proj = h @ w_in[l]
        (cv_a, cv_g, hg_q, hg_f, hg_i, hg_g, sb_q, sb_k, sb_v, gl) = jnp.split(proj, SPLIT_IDX, axis=-1)
        y_conv = conv_branch(cv_a, cv_g, conv_w[l], conv_b[l], conv_ln_g[l], conv_ln_b[l], w_conv_proj[l])
        y_hgrn = hgrn2_branch(hg_q, hg_f, hg_i, hg_g, lower_bounds[l], hgrn_norm_g[l], w_hgrn_proj[l])
        y_sb = stick_breaking_branch(sb_q, sb_k, sb_v, sb_qn_g[l], sb_kn_g[l], w_sb_proj[l])
        gates = jax.nn.sigmoid(gl + gate_b[l]).reshape(B, S, N_BRANCH, D)
        merged = gates[:, :, 0] * y_conv + gates[:, :, 1] * y_hgrn + gates[:, :, 2] * y_sb
        x = x + g1 * (merged @ w_out[l])

        h2 = rms_norm(x, norm2_g[l]) * (1.0 + sc2) + sh2
        x = x + g2 * (jnp.square(jax.nn.relu(h2 @ mlp_w1[l])) @ mlp_w2[l])
    return x


_first_inputs = first_inputs


def first_inputs(seed=0):
    import zlib

    import numpy as np

    out = dict(_first_inputs(seed))
    spreads = {}
    factors = {}
    for name, (base, spread) in spreads.items():
        noise = np.random.default_rng([zlib.crc32(name.encode()), seed]).standard_normal(out[name].shape)
        drawn = base * np.exp(spread * noise) if base else spread * noise
        out[name] = __import__('jax').numpy.asarray(drawn.astype(out[name].dtype))
    for name, factor in factors.items():
        out[name] = (out[name] * factor).astype(out[name].dtype)
    return out


_narrow_inputs = first_inputs


def first_inputs(seed=0):

    out = dict(_narrow_inputs(seed))
    wider = {'mod_b': 4.08,
     'norm1_g': 12.0,
     'gate_b': 12.0,
     'conv_b': 12.0,
     'conv_ln_g': 12.0,
     'conv_ln_b': 12.0,
     'hgrn_norm_g': 12.0,
     'sb_qn_g': 12.0,
     'sb_kn_g': 12.0,
     'norm2_g': 7.28}
    for name, times in wider.items():
        mean = out[name].mean()
        out[name] = (mean + times * (out[name] - mean)).astype(out[name].dtype)
    return out


DEPTH_2 = 2

N_HEADS = 8
HEAD_DIM = 128
D_ATTN = N_HEADS * HEAD_DIM
Q_BLOCK = 128
FORGET_BIAS = 2.0
D_RNN = D_MODEL
N_RNN_BLOCKS = 16
RNN_BLOCK = D_RNN // N_RNN_BLOCKS
CONV_WIDTH_2 = 4
LRU_C = 8.0
D_FF_2 = 2816
NORM_EPS = 1e-6

SPLIT_POINTS = (
    D_ATTN,
    2 * D_ATTN,
    3 * D_ATTN,
    3 * D_ATTN + N_HEADS,
    3 * D_ATTN + N_HEADS + D_RNN,
    3 * D_ATTN + N_HEADS + 2 * D_RNN,
    3 * D_ATTN + N_HEADS + 2 * D_RNN + D_MODEL,
)
N_IN = 3 * D_ATTN + N_HEADS + 2 * D_RNN + 2 * D_MODEL


def rms_norm_2(x, g):
    xf = x.astype(jnp.float32)
    y = xf * lax.rsqrt(jnp.mean(xf * xf, axis=-1, keepdims=True) + NORM_EPS)
    return (y * g.astype(jnp.float32)).astype(x.dtype)

def swiglu(x, w_gate, w_up, w_down):
    return (jax.nn.silu(x @ w_gate) * (x @ w_up)) @ w_down

def forgetting_attention(q, k, v, log_f):
    B, S = q.shape[0], q.shape[1]
    nb = S // Q_BLOCK
    scale = HEAD_DIM ** -0.5
    c = jnp.cumsum(log_f, axis=1).transpose(0, 2, 1)
    q = q.transpose(0, 2, 1, 3)
    k = k.transpose(0, 2, 1, 3)
    v = v.transpose(0, 2, 1, 3)
    qb = q.reshape(B, N_HEADS, nb, Q_BLOCK, HEAD_DIM).transpose(2, 0, 1, 3, 4)
    cb = c.reshape(B, N_HEADS, nb, Q_BLOCK).transpose(2, 0, 1, 3)
    k_pos = jnp.arange(S)

    def one_block(args):
        q_i, c_i, i = args
        s = jnp.einsum('bhqd,bhkd->bhqk', q_i, k).astype(jnp.float32) * scale
        s = s + (c_i[..., :, None] - c[:, :, None, :])
        q_pos = i * Q_BLOCK + jnp.arange(Q_BLOCK)
        mask = k_pos[None, :] <= q_pos[:, None]
        s = jnp.where(mask, s, -jnp.inf)
        p = jax.nn.softmax(s, axis=-1)
        return jnp.einsum('bhqk,bhkd->bhqd', p.astype(v.dtype), v)

    out = lax.map(one_block, (qb, cb, jnp.arange(nb)))
    return out.transpose(1, 0, 3, 2, 4).reshape(B, S, D_ATTN)

def causal_depthwise_conv(x, w, b):
    S = x.shape[1]
    xp = jnp.pad(x, ((0, 0), (CONV_WIDTH_2 - 1, 0), (0, 0)))
    y = b
    for tap in range(CONV_WIDTH_2):
        y = y + xp[:, tap:tap + S, :] * w[tap]
    return y

def block_diag_linear(x, w, b):
    B, S = x.shape[0], x.shape[1]
    xb = x.reshape(B, S, N_RNN_BLOCKS, RNN_BLOCK)
    return jnp.einsum('bsnc,ncd->bsnd', xb, w).reshape(B, S, D_RNN) + b

def rg_lru(x, w_a, b_a, w_x, b_x, lam):
    xf = x.astype(jnp.float32)
    r = jax.nn.sigmoid(block_diag_linear(x, w_a, b_a).astype(jnp.float32))
    i = jax.nn.sigmoid(block_diag_linear(x, w_x, b_x).astype(jnp.float32))
    log_a = -LRU_C * r * jax.nn.softplus(-lam.astype(jnp.float32))
    a = jnp.exp(log_a)
    u = jnp.sqrt(-jnp.expm1(2.0 * log_a)) * (i * xf)

    def combine(left, right):
        a1, b1 = left
        a2, b2 = right
        return a1 * a2, a2 * b1 + b2

    _, h = lax.associative_scan(combine, (a, u), axis=1)
    return h.astype(x.dtype)

def second_inputs(seed: int = 0) -> dict:
    key = jax.random.key(seed)
    ks = jax.random.split(key, 24)
    L, D, F = DEPTH_2, D_MODEL, D_FF_2
    nrm = lambda k, shape, fan_in: jax.random.normal(k, shape, jnp.float32) * (fan_in ** -0.5)
    gain = lambda k, shape: 1.0 + 0.02 * jax.random.normal(k, shape, jnp.float32)
    bias = lambda k, shape: 0.02 * jax.random.normal(k, shape, jnp.float32)

    x = jax.random.normal(ks[0], (BATCH, SEQ, D), jnp.float32)
    b_in = bias(ks[6], (L, N_IN))
    b_in = b_in.at[:, SPLIT_POINTS[2]:SPLIT_POINTS[3]].add(FORGET_BIAS)
    u = jax.random.uniform(ks[15], (L, D_RNN), jnp.float32, 0.9, 0.999)
    lru_lambda = jnp.log(u) - jnp.log1p(-u)
    return {
        "x": x,
        "ffn1_norm": gain(ks[1], (L, D)),
        "ffn1_w_gate": nrm(ks[2], (L, D, F), D),
        "ffn1_w_up": nrm(ks[3], (L, D, F), D),
        "ffn1_w_down": nrm(ks[4], (L, F, D), F),
        "mix_norm": gain(ks[5], (L, D)),
        "w_in": nrm(ks[7], (L, D, N_IN), D),
        "b_in": b_in,
        "q_norm": gain(ks[8], (L, HEAD_DIM)),
        "k_norm": gain(ks[9], (L, HEAD_DIM)),
        "conv_w": nrm(ks[10], (L, CONV_WIDTH_2, D_RNN), CONV_WIDTH_2),
        "conv_b": bias(ks[11], (L, D_RNN)),
        "lru_w_a": nrm(ks[12], (L, N_RNN_BLOCKS, RNN_BLOCK, RNN_BLOCK), RNN_BLOCK),
        "lru_b_a": bias(ks[13], (L, D_RNN)),
        "lru_w_x": nrm(ks[14], (L, N_RNN_BLOCKS, RNN_BLOCK, RNN_BLOCK), RNN_BLOCK),
        "lru_b_x": bias(ks[16], (L, D_RNN)),
        "lru_lambda": lru_lambda,
        "w_o_attn": nrm(ks[17], (L, D_ATTN, D), D_ATTN),
        "w_o_rnn": nrm(ks[18], (L, D_RNN, D), D_RNN),
        "w_out": nrm(ks[19], (L, D, D), D),
        "ffn2_norm": gain(ks[20], (L, D)),
        "ffn2_w_gate": nrm(ks[21], (L, D, F), D),
        "ffn2_w_up": nrm(ks[22], (L, D, F), D),
        "ffn2_w_down": nrm(ks[23], (L, F, D), F),
    }

def second_block(x, ffn1_norm, ffn1_w_gate, ffn1_w_up, ffn1_w_down, mix_norm, w_in, b_in,
              q_norm, k_norm, conv_w, conv_b, lru_w_a, lru_b_a, lru_w_x, lru_b_x, lru_lambda,
              w_o_attn, w_o_rnn, w_out, ffn2_norm, ffn2_w_gate, ffn2_w_up, ffn2_w_down):
    B, S = x.shape[0], x.shape[1]
    for l in range(DEPTH_2):
        x = x + 0.5 * swiglu(rms_norm_2(x, ffn1_norm[l]), ffn1_w_gate[l], ffn1_w_up[l], ffn1_w_down[l])

        h = rms_norm_2(x, mix_norm[l])
        proj = h @ w_in[l] + b_in[l]
        q, k, v, f_logit, xr, gr, g_attn, g_rnn = jnp.split(proj, SPLIT_POINTS, axis=-1)

        q = rms_norm_2(q.reshape(B, S, N_HEADS, HEAD_DIM), q_norm[l])
        k = rms_norm_2(k.reshape(B, S, N_HEADS, HEAD_DIM), k_norm[l])
        v = v.reshape(B, S, N_HEADS, HEAD_DIM)
        log_f = jax.nn.log_sigmoid(f_logit.astype(jnp.float32))
        y_attn = forgetting_attention(q, k, v, log_f) @ w_o_attn[l]

        xr = causal_depthwise_conv(xr, conv_w[l], conv_b[l])
        yr = rg_lru(xr, lru_w_a[l], lru_b_a[l], lru_w_x[l], lru_b_x[l], lru_lambda[l]) * jax.nn.gelu(gr)
        y_rnn = yr @ w_o_rnn[l]

        merged = jax.nn.sigmoid(g_attn) * y_attn + jax.nn.sigmoid(g_rnn) * y_rnn
        x = x + merged @ w_out[l]

        x = x + 0.5 * swiglu(rms_norm_2(x, ffn2_norm[l]), ffn2_w_gate[l], ffn2_w_up[l], ffn2_w_down[l])
    return x


def setup_inputs(seed=0):
    out = dict(first_inputs(seed))
    for name, value in second_inputs(seed + 1).items():
        if name != "x":
            out[name + "_2"] = value
    return out


def reference(
    x, c, mod_w, mod_b, norm1_g, w_in, gate_b, conv_w, conv_b, conv_ln_g, conv_ln_b,
    w_conv_proj, hgrn_lb, hgrn_norm_g, w_hgrn_proj, sb_qn_g, sb_kn_g, w_sb_proj, w_out, norm2_g,
    mlp_w1, mlp_w2, ffn1_norm_2, ffn1_w_gate_2, ffn1_w_up_2, ffn1_w_down_2, mix_norm_2, w_in_2,
    b_in_2, q_norm_2, k_norm_2, conv_w_2, conv_b_2, lru_w_a_2, lru_b_a_2, lru_w_x_2, lru_b_x_2,
    lru_lambda_2, w_o_attn_2, w_o_rnn_2, w_out_2, ffn2_norm_2, ffn2_w_gate_2, ffn2_w_up_2,
    ffn2_w_down_2,
):
    x = first_block(
        x, c, mod_w, mod_b, norm1_g, w_in, gate_b, conv_w, conv_b, conv_ln_g, conv_ln_b,
        w_conv_proj, hgrn_lb, hgrn_norm_g, w_hgrn_proj, sb_qn_g, sb_kn_g, w_sb_proj, w_out,
        norm2_g, mlp_w1, mlp_w2,
    )
    return second_block(
        x, ffn1_norm_2, ffn1_w_gate_2, ffn1_w_up_2, ffn1_w_down_2, mix_norm_2, w_in_2, b_in_2,
        q_norm_2, k_norm_2, conv_w_2, conv_b_2, lru_w_a_2, lru_b_a_2, lru_w_x_2, lru_b_x_2,
        lru_lambda_2, w_o_attn_2, w_o_rnn_2, w_out_2, ffn2_norm_2, ffn2_w_gate_2, ffn2_w_up_2,
        ffn2_w_down_2,
    )


_drawn_inputs = setup_inputs


def setup_inputs(seed=0):
    import zlib

    import numpy as np

    out = dict(_drawn_inputs(seed))
    spreads = {}
    factors = {'gate_b': 4.997,
     'conv_ln_b': 3.172,
     'sb_qn_g': 4.384,
     'sb_kn_g': 3.059,
     'ffn1_norm_2': 4.953,
     'mix_norm_2': 4.656,
     'q_norm_2': 8.0,
     'k_norm_2': 8.0,
     'conv_b_2': 2.959,
     'lru_b_a_2': 8.0,
     'lru_b_x_2': 8.0,
     'ffn2_norm_2': 5.709}
    for name, (base, spread) in spreads.items():
        noise = np.random.default_rng([zlib.crc32(name.encode()), seed]).standard_normal(out[name].shape)
        drawn = base * np.exp(spread * noise) if base else spread * noise
        out[name] = __import__('jax').numpy.asarray(drawn.astype(out[name].dtype))
    for name, factor in factors.items():
        out[name] = (out[name] * factor).astype(out[name].dtype)
    return out
```

```python
from contextlib import ExitStack, contextmanager

import concourse.bass as bass
from concourse import mybir

F32 = mybir.dt.float32
F32R = mybir.dt.float32r
I8 = mybir.dt.int8
ALU = mybir.AluOpType
ACT = mybir.ActivationFunctionType
AX_X = mybir.AxisListType.X

P = 128
S = 512
D = 1024
KT = D // P
TT = S // P
RING = 4
MODS = 6 * KT
MOD_RING = 8
CONV_CH = 512
CT = CONV_CH // P
TAPS = 31
PAD = TAPS - 1
HG_HEADS = 4
SB_HEADS = 8
SB_DH = 64
MLP_CHUNKS = 4 * D // (2 * P)
LAYERS = 2
HEADS = 8
TAPS_2 = 4
FFN_CHUNKS = 2816 // (2 * P)
LRU_C = 8.0
EPS = 1e-6
NEG = -1e30
LEVELS = (256, 128, 64, 32, 16, 8, 4, 2, 1)
BESIDE = [(0, 1), (2, 3), (4,), (5, 6), (7, 8, 9)]
V_TILES = (4 + 4 * 2 * 3 + 4 + 8 + 8 * MLP_CHUNKS) + LAYERS * (2 * 10 * FFN_CHUNKS + 8 + 8 + 8 + 8)
PER_LAYER = {"pe": {"rt": 19, "aux": 4, "sq": 40, "dve": 252, "units": 212, "op": 48, "tiles": 352, "act": 100, "conv": 4, "hid": 44, "wf": 1, "fc": 1, "lru": 16, "cum": 1, "sc": 32, "turn": 32, "pv": 32}, "act": {"sq": 40, "rt": 19, "tiles": 352, "t": 40, "units": 212, "dve": 252, "act": 100, "merged": 8, "op": 48, "par": 16, "conv": 4, "f": 1, "gates": 4, "spl": 1, "root": 4, "exp": 32, "turn": 32}, "dve": {"rt": 19, "t": 40, "rounded": 48, "tiles": 352, "dve": 252, "act": 100, "par": 16, "spl": 1, "cum": 1, "lru": 4, "sc": 32, "pr": 32}}
UNITS = (60 + 12 + 8 + 64) + LAYERS * (2 * 66 + 16 + 24 + 16 + 16 + 8)
LEAD = 3

PAR1 = {}
for _name, _n in (("c", KT), ("mod_b", MODS), ("norm1_g", KT), ("gate_b", 3 * KT), ("conv_w", TAPS * CT), ("conv_b", CT),
                  ("ln_g", CT), ("ln_b", CT), ("lb", HG_HEADS), ("hg_g", 1), ("sbq_g", 1), ("sbk_g", 1), ("norm2_g", KT)):
    PAR1[_name] = (sum(n for _, n in PAR1.values()), _n)
N_PAR1 = sum(n for _, n in PAR1.values())
PAR2 = {}
for _name, _n in (("ffn1_g", KT), ("mix_g", KT), ("ffn2_g", KT), ("b_q", KT), ("b_k", KT), ("b_v", KT), ("b_f", 1), ("b_xr", KT),
                  ("b_gr", KT), ("b_ga", KT), ("b_gn", KT), ("q_g", 1), ("k_g", 1), ("conv_w", TAPS_2 * KT), ("conv_b", KT),
                  ("b_a", KT), ("b_x", KT), ("lam", KT), ("w_f", KT * HEADS)):
    PAR2[_name] = (sum(n for _, n in PAR2.values()), _n)
N_PAR2 = sum(n for _, n in PAR2.values())


class Count:

    def __init__(self):
        self.n = 0
        self.turns = []

    def at(self, more=0):
        value = self.n + more
        for register, per in self.turns:
            value = register * per + value
        return value

    def quarter(self, more):
        value = 16 * ((self.n + more) // RING + 1)
        for register, per in self.turns:
            value = register * (16 * per // RING) + value
        return value


class Counts:

    def __init__(self):
        self.a = Count()
        self.act = Count()
        self.arg = Count()
        self.aux = Count()
        self.conv = Count()
        self.cum = Count()
        self.decay = Count()
        self.dve = Count()
        self.exp = Count()
        self.f = Count()
        self.fc = Count()
        self.gates = Count()
        self.hid = Count()
        self.level = Count()
        self.log = Count()
        self.lru = Count()
        self.merged = Count()
        self.mod = Count()
        self.op = Count()
        self.par = Count()
        self.pr = Count()
        self.pv = Count()
        self.ready = Count()
        self.root = Count()
        self.rounded = Count()
        self.rt = Count()
        self.sc = Count()
        self.spl = Count()
        self.sq = Count()
        self.t = Count()
        self.tiles = Count()
        self.turn = Count()
        self.units = Count()
        self.wf = Count()
        self.z = Count()
        self.named = {"a": self.a, "act": self.act, "arg": self.arg, "aux": self.aux, "conv": self.conv, "cum": self.cum,
                      "decay": self.decay, "dve": self.dve, "exp": self.exp, "f": self.f, "fc": self.fc, "gates": self.gates, "hid":
                      self.hid, "level": self.level, "log": self.log, "lru": self.lru, "merged": self.merged, "mod": self.mod, "op":
                      self.op, "par": self.par, "pr": self.pr, "pv": self.pv, "ready": self.ready, "root": self.root, "rounded":
                      self.rounded, "rt": self.rt, "sc": self.sc, "spl": self.spl, "sq": self.sq, "t": self.t, "tiles": self.tiles, "turn":
                      self.turn, "units": self.units, "wf": self.wf, "z": self.z}




@contextmanager
def loop(eng, trips, counts, **per):
    before = {k: v.n for k, v in counts.named.items()}
    with eng.Fori(0, trips) as i:
        for name, n in per.items():
            counts.named[name].turns.append((i, n))
        yield i
        went = {k: v.n - before.get(k, 0) for k, v in counts.named.items() if v.n != before.get(k, 0)}
        assert went == {k: n for k, n in per.items() if n}, went
        for name in per:
            counts.named[name].turns.pop()
    for name, n in per.items():
        counts.named[name].n += (trips - 1) * n


def need(eng, sem, value):
    if not isinstance(value, int) or value > 0:
        eng.wait_ge(sem, value)


def build(nc, x_t, par1, par2, lru, mod_w, stream, out_t):
    with ExitStack() as ctx:
        def sb(name, shape, dt=F32):
            return ctx.enter_context(nc.sbuf_tensor(name, shape, dt))

        def sem(name):
            return ctx.enter_context(nc.semaphore(name))

        ps = ctx.enter_context(nc.psum_tensor("ps", [P, 8, S], F32))
        raw = sb("raw", [P, RING, D])
        w_hi = sb("w_hi", [P, RING, D], F32R)
        w_lo = sb("w_lo", [P, RING, D], F32R)
        a_hi, a_lo = sb("a_hi", [P, KT, S], F32R), sb("a_lo", [P, KT, S], F32R)
        b_hi, b_lo = sb("b_hi", [P, KT, S], F32R), sb("b_lo", [P, KT, S], F32R)
        xres = sb("xres", [P, KT, S])
        params = sb("params", [P, max(N_PAR1, N_PAR2)])
        cols = sb("cols", [P, 128])
        ident = sb("ident", [P, P])
        ones = sb("ones", [P, S])
        pair_ones = sb("pair_ones", [P, P])
        neg_tri = sb("neg_tri", [P, P])
        neg_ones = sb("neg_ones", [P, P])
        before = sb("before", [P, P])
        hide_ge = sb("hide_ge", [P, P])
        hide_gt = sb("hide_gt", [P, P])
        masks = sb("masks", [P, 8, P], I8)
        sgate = sb("sgate", [P, 2, S])
        row_tile = sb("row_tile", [P, S])
        ARENA = 17160
        arena = sb("arena", [P, ARENA])

        def area(at, *dims):
            n = 1
            for d in dims:
                n *= d
            assert at + n <= ARENA
            flat = arena[:, at:at + n]
            if len(dims) == 1:
                return flat
            names = "abc"[:len(dims)]
            return flat.rearrange(f"p ({' '.join(names)}) -> p {' '.join(names)}", **dict(zip(names, dims)))

        def par(table, name, i=0, n=1):
            at, size = table[name]
            assert i + n <= size
            return params[:, at + i:at + i + n]

        c_act = cols[:, 0:8]
        modp = cols[:, 8:56]
        scale1 = cols[:, 56:64]
        scale2 = cols[:, 64:72]
        keep = cols[:, 72:76]
        q_col = cols[:, 76:77]
        eps_col = cols[:, 77:78]
        one_col = cols[:, 78:79]
        spl = cols[:, 80:88]
        half_spl = cols[:, 88:96]
        half_ba = cols[:, 96:104]
        half_bx = cols[:, 104:112]
        tmp8 = cols[:, 112:120]
        ones_p = ones[:, 0:P]

        N0 = ARENA - 5 * S
        sq, rt, tt = area(N0, 2, S), area(N0 + 2 * S, S), area(N0 + 3 * S, 2, S)

        U0, C0 = 0, CT * (PAD + S)
        D0 = C0 + CT * S
        Q0 = D0 + 16 * S
        assert Q0 + 4 * S <= N0
        conv_in, conv_out = area(U0, CT, PAD + S), area(C0, CT, S)
        hg_q, hg_k, hg_v, hg_g = (area(D0 + i * 4 * S, 4, S) for i in range(4))
        mod_stage = area(U0, MOD_RING, D)
        hg_b64, hg_b256 = area(0, S), area(S, S)
        hg_e, hg_qe, hg_ke = area(2 * S, 2, S), area(4 * S, 2, S), area(6 * S, 2, S)
        hg_log = hg_qe[:, 1, :]
        assert 8 * S <= D0
        hg_s, hg_p256, hg_p128 = area(Q0, TT, P), area(Q0 + S, 2, 256), area(Q0 + 2 * S, 2, P)
        sb_q, sb_k, sb_v = area(Q0, 4, S), hg_q, hg_v
        SB_W = [S - P * j for j in range(TT)]
        SB_AT = [sum(SB_W[:j]) for j in range(TT)]
        sb_a = [[area(i * sum(SB_W) + SB_AT[j], SB_W[j]) for j in range(TT)] for i in range(2)]
        sb_sp = [[area(D0 + (1 + 2 * i) * 4 * S + SB_AT[j], SB_W[j]) for j in range(TT)] for i in range(2)]
        sb_e = [area(2 * sum(SB_W) + i * S, S) for i in range(2)]
        sb_diag = [area(2 * sum(SB_W) + 2 * S + i * P, P) for i in range(2)]
        assert 2 * sum(SB_W) + 2 * S + 2 * P <= D0
        reset64 = row_tile[:, :]

        R0 = 4 * S
        lru_w = area(0, 2, KT, P)
        XW = TAPS_2 - 1 + S + 1
        xr = area(R0, 2, XW)
        gr = area(R0 + 2 * XW, 2, 2, S)
        RT = R0 + 2 * XW + 4 * S
        xc, rr, ii, th = (area(RT + i * 2 * S, 2, S) for i in range(4))
        QKV = 6 * S
        merged2 = area(R0, KT, S)
        qkv_at = [RT + 8 * S, R0 + KT * S]
        assert qkv_at[1] + QKV <= qkv_at[0]
        q_h = [area(at, 2, S) for at in qkv_at]
        k_h = [area(at + 2 * S, 2, S) for at in qkv_at]
        v_h = [area(at + 4 * S, TT, 2 * P) for at in qkv_at]
        T0 = qkv_at[0] + QKV
        probs = area(T0, 2, S)
        probs_t = area(0, TT, S)
        f_tok = area(T0 + 2 * S, TT, HEADS)
        neg_max, den = area(T0 + 2 * S + 32, 2), area(T0 + 2 * S + 34, 2)
        assert T0 + 2 * S + 64 <= N0
        neg_cum_f = row_tile[0:HEADS, :]
        f_row, f_abs = tt[0:HEADS, 0, :], tt[0:HEADS, 1, :]
        wf_hi, wf_lo = sb("wf_hi", [P, KT, HEADS], F32R), sb("wf_lo", [P, KT, HEADS], F32R)

        par_loaded, x_loaded, lru_loaded, out_stored = sem("par_loaded"), sem("x_loaded"), sem("lru_loaded"), sem("out_stored")
        mod_loaded = [sem(f"mod_loaded{i}") for i in range(MOD_RING)]
        raw_loaded = [sem(f"raw_loaded{i}") for i in range(RING)]
        mod_used, c_ready, consts_ready = sem("mod_used"), sem("c_ready"), sem("consts_ready")
        hi_ready, lo_ready = sem("hi_ready"), sem("lo_ready")
        tiles_done, act_evacuated, dve_evacuated, aux_evacuated = (
            sem("tiles_done"), sem("act_evacuated"), sem("dve_evacuated"), sem("aux_evacuated"))
        sq_ready, stat_done, rt_ready, normalised = sem("sq_ready"), sem("stat_done"), sem("rt_ready"), sem("normalised")
        t_ready, op_rounded, op_ready, hidden_ready = sem("t_ready"), sem("op_rounded"), sem("op_ready"), sem("hidden_ready")
        conv_ready, mean_done, centred, merged_ready = sem("conv_ready"), sem("mean_done"), sem("centred"), sem("merged_ready")
        keep_asked, keep_ready, log_asked, log_ready = sem("keep_asked"), sem("keep_ready"), sem("log_asked"), sem("log_ready")
        decay_asked, decay_ready, level_ready, level_done, level_merged, head_done = (
            sem("decay_asked"), sem("decay_ready"), sem("level_ready"), sem("level_done"), sem("level_merged"), sem("head_done"))
        z_done, log1p_ready, sp_ready, arg_done, diag_ready, a_ready = (
            sem("z_done"), sem("log1p_ready"), sem("sp_ready"), sem("arg_done"), sem("diag_ready"), sem("a_ready"))
        spl_asked, spl_logged, spl_ready, wf_rounded, wf_ready = (
            sem("spl_asked"), sem("spl_logged"), sem("spl_ready"), sem("wf_rounded"), sem("wf_ready"))
        f_done, f_copied, f_turned, f_asked, f_logged, cum_ready = (
            sem("f_done"), sem("f_copied"), sem("f_turned"), sem("f_asked"), sem("f_logged"), sem("cum_ready"))
        gates_done, lru_ready, root_asked, root_ready = sem("gates_done"), sem("lru_ready"), sem("root_asked"), sem("root_ready")
        scores_done, max_ready, exp_ready, probs_ready, turned, turned_copied = (
            sem("scores_done"), sem("max_ready"), sem("exp_ready"), sem("probs_ready"), sem("turned"), sem("turned_copied"))

        block = ctx.enter_context(nc.Block())

        @block.sync
        def _(sp):
            sp.dma_start(params[:, 0:N_PAR1], par1).then_inc(par_loaded, 16)
            sp.dma_start(xres[:, :, :], x_t).then_inc(x_loaded, 16)
            for s in range(MOD_RING):
                sp.dma_start(mod_stage[:, s, :], mod_w[s]).then_inc(mod_loaded[s], 16)
            with sp.Fori(1, MODS // MOD_RING) as i:
                for s in range(MOD_RING):
                    sp.wait_ge(mod_used, i * MOD_RING + (s + 1 - MOD_RING))
                    sp.dma_start(mod_stage[:, s, :], mod_w[bass.ds(i * MOD_RING + s, 1)].rearrange("o p n -> p (o n)")
                                 ).then_inc(mod_loaded[s], 16)
            for s in range(RING):
                sp.dma_start(raw[:, s, :], stream[s]).then_inc(raw_loaded[s], 16)
            with sp.Fori(1, UNITS // RING + 1) as i:
                for s in range(RING):
                    sp.wait_ge(lo_ready, i * RING + (s + 1 - RING))
                    sp.dma_start(raw[:, s, :], stream[bass.ds(i * RING + s, 1)].rearrange("o p n -> p (o n)")
                                 ).then_inc(raw_loaded[s], 16)
            sp.wait_ge(dve_evacuated, V_TILES)
            sp.dma_start(out_t, xres[:, :, :]).then_inc(out_stored, 16)
            for s in range(RING):
                sp.wait_ge(raw_loaded[s], 16 * (UNITS // RING + 1))
            sp.wait_ge(out_stored, 16)

        @block.gpsimd
        def _(pool):
            pool.memset(ones[:, :], 1.0)
            pool.memset(neg_ones[:, :], -1.0)
            pool.memset(neg_tri[:, :], -1.0)
            pool.memset(before[:, :], 1.0)
            for t in (ident, hide_ge, hide_gt, pair_ones):
                pool.memset(t[:, :], 0.0)
            pool.memset(masks[:, :, :], 0)
            pool.memset(reset64, 1.0)
            pool.memset(cols[:, :], 0.0)
            pool.drain()
            pool.memset(eps_col, EPS)
            pool.memset(one_col, 1.0)
            pool.memset(reset64.rearrange("p (c t) -> p c t", t=64)[:, :, 0:1], 0.0)
            pool.drain()
            pool.memset(pair_ones[0:64, 0:64], 1.0)
            pool.drain()
            pool.memset(pair_ones[64:128, 64:128], 1.0)
            pool.drain()
            pool.affine_select(out=ident[:, :], in_=ident[:, :], compare_op=ALU.not_equal, fill=1.0, base=0,
                               pattern=[[-1, P]], channel_multiplier=1)
            pool.affine_select(out=neg_tri[:, :], in_=neg_tri[:, :], compare_op=ALU.is_ge, fill=0.0, base=0,
                               pattern=[[-1, P]], channel_multiplier=1)
            pool.affine_select(out=hide_gt[:, :], in_=hide_gt[:, :], compare_op=ALU.is_ge, fill=NEG, base=0,
                               pattern=[[-1, P]], channel_multiplier=1)
            pool.affine_select(out=before[:, :], in_=before[:, :], compare_op=ALU.is_gt, fill=0.0, base=0,
                               pattern=[[1, P]], channel_multiplier=-1)
            pool.affine_select(out=hide_ge[:, :], in_=hide_ge[:, :], compare_op=ALU.is_gt, fill=NEG, base=0,
                               pattern=[[1, P]], channel_multiplier=-1)
            pool.affine_select(out=masks[:, 7, :], in_=masks[:, 7, :], compare_op=ALU.not_equal, fill=1.0, base=0,
                               pattern=[[-1, P]], channel_multiplier=1)
            halves = [(m, masks[:, n, :].rearrange("p (b h i) -> p b h i", h=2, i=m)[:, :, 1, :]) for n, m in enumerate(LEVELS[2:])]
            for m, second in halves:
                pool.memset(second, 1)
            pool.drain()
            for m, second in halves:
                pool.affine_select(out=second, in_=second, compare_op=ALU.is_ge, fill=0.0, base=0,
                                   pattern=[[-2 * m, P // (2 * m)], [0, m]], channel_multiplier=1)
            pool.drain()
            for m, second in halves:
                pool.affine_select(out=second, in_=second, compare_op=ALU.is_ge, fill=0.0, base=m - 1,
                                   pattern=[[2 * m, P // (2 * m)], [0, m]], channel_multiplier=-1)
            pool.drain()
            pool.memset(cols[:, 127:128], 0.0).then_inc(consts_ready, 1)
            with pool.Fori(0, UNITS // RING) as i:
                for s in range(RING):
                    pool.wait_ge(hi_ready, i * RING + (s + 1))
                    pool.tensor_tensor(w_lo[:, s, :], raw[:, s, :], w_hi[:, s, :].bitcast(F32), ALU.subtract).then_inc(lo_ready, 1)

        @block.tensor
        def _(pe):
            c = Counts()

            def mm3(out, hi, lo, x_hi, x_lo, start, stop):
                pe.matmul(out, lo, x_hi, start=start, stop=False)
                pe.matmul(out, hi, x_lo, start=False, stop=False)
                return pe.matmul(out, hi, x_hi, start=False, stop=stop)

            def unit():
                pe.wait_ge(lo_ready, c.units.at(1))
                c.units.n += 1
                return (c.units.n - 1) % RING

            def bank_a():
                need(pe, act_evacuated, c.act.at(-1))
                c.act.n += 1
                return (c.act.n - 1) % 2

            def bank_v():
                need(pe, dve_evacuated, c.dve.at(-1))
                c.dve.n += 1
                return 2 + (c.dve.n - 1) % 2

            def tile(last):
                last.then_inc(tiles_done, 1)
                c.tiles.n += 1

            def project(bank, fresh=False):
                s = unit()
                for k in range(KT):
                    if fresh:
                        pe.wait_ge(op_ready, c.op.at(k + 1))
                    w = slice(k * P, k * P + P)
                    last = mm3(ps[:, bank, :], w_hi[:, s, w], w_lo[:, s, w], a_hi[:, k, :], a_lo[:, k, :], k == 0, k == KT - 1)
                if fresh:
                    c.op.n += KT
                tile(last)

            def project_half(first):
                s = unit()
                for m in range(2):
                    bank = bank_v()
                    for k in range(4):
                        w = slice(k * 2 * P + m * P, k * 2 * P + m * P + P)
                        last = mm3(ps[:, bank, :], w_hi[:, s, w], w_lo[:, s, w], b_hi[:, first + k, :], b_lo[:, first + k, :],
                                   k == 0, k == 3)
                    tile(last)

            def project_b():
                s = unit()
                bank = bank_v()
                for k in range(KT):
                    w = slice(k * P, k * P + P)
                    last = mm3(ps[:, bank, :], w_hi[:, s, w], w_lo[:, s, w], b_hi[:, k, :], b_lo[:, k, :], k == 0, k == KT - 1)
                tile(last)

            def down(half):
                pe.wait_ge(hidden_ready, c.hid.at(2))
                c.hid.n += 2
                for _ in range(2):
                    s = unit()
                    for m in range(4):
                        bank = bank_v()
                        for k in range(2):
                            w = slice(k * 4 * P + m * P, k * 4 * P + m * P + P)
                            last = mm3(ps[:, bank, :], w_hi[:, s, w], w_lo[:, s, w], b_hi[:, 2 * half + k, :], b_lo[:, 2 * half + k, :],
                                       k == 0, k == 1)
                        tile(last)

            def stats(n, weights=ones_p):
                need(pe, rt_ready, c.rt.at(0))
                need(pe, aux_evacuated, c.aux.at(0))
                for k in range(n):
                    pe.wait_ge(sq_ready, c.sq.at(1))
                    pe.matmul(ps[:, 7, :], weights, sq[:, c.sq.n % 2, :], start=k == 0, stop=k == n - 1).then_inc(stat_done, 1)
                    c.sq.n += 1
                c.rt.n += 1

            def values_4(first):
                need(pe, aux_evacuated, c.aux.at(0))
                for u in range(4):
                    s = unit()
                    for t in range(TT):
                        for k in range(2):
                            w, f, tok = slice(k * S, k * S + S), 2 * u + k, slice(t * P, t * P + P)
                            start, stop = u == 0 and k == 0, u == 3 and k == 1
                            pe.matmul(ps[:, 4 + t, :], a_hi[:, f, tok], w_lo[:, s, w], start=start, stop=False)
                            pe.matmul(ps[:, 4 + t, :], a_lo[:, f, tok], w_hi[:, s, w], start=False, stop=False)
                            last = pe.matmul(ps[:, 4 + t, :], a_hi[:, f, tok], w_hi[:, s, w], start=False, stop=stop)
                    tile(last)
                c.aux.n += 1

            pe.wait_ge(consts_ready, 1)
            pe.wait_ge(c_ready, 1)
            stats(KT)
            with loop(pe, MODS // MOD_RING, c, mod=MOD_RING) as i:
                for s in range(MOD_RING):
                    pe.wait_ge(mod_loaded[s], i * 16 + 16)
                    for k in range(KT):
                        last = pe.matmul(ps[:, 6, bass.ds(i * MOD_RING + s, 1)], mod_stage[:, s, k * P:k * P + P], c_act[:, k:k + 1],
                                         start=k == 0, stop=k == KT - 1)
                    last.then_inc(mod_used, 1)
                    c.mod.n += 1

            for j in range(CT):
                project(bank_v(), fresh=j == 0)
                project(bank_a())
            for h in range(2 * HG_HEADS):
                project(bank_a())
            values_4(0)
            for h in range(HG_HEADS):
                project(bank_a())

            def gates():
                project(bank_a())
                project(bank_a())

            def hgrn_head(h):
                def done(last):
                    last.then_inc(level_done, 1)
                    c.level.n += 1

                for n, m in enumerate(LEVELS + (0,)):
                    bank = 4 + c.level.n % 2
                    if m:
                        pe.wait_ge(level_ready, c.ready.at(1))
                        c.ready.n += 1
                    need(pe, level_merged, c.level.at(-1))
                    ke, qe = (hg_ke[:, n % 2, :], hg_qe[:, n % 2, :]) if m else (hg_k[:, h, :], hg_q[:, h, :])
                    if m == 256:
                        for j in range(2):
                            last = pe.matmul(ps[:, bank, j * 256:j * 256 + 256], ke[:, j * P:j * P + P], qe[:, 256:512], start=True, stop=True)
                    elif m == 128:
                        for j in range(2):
                            last = pe.matmul(ps[:, bank, j * P:j * P + P], ke[:, 2 * j * P:2 * j * P + P],
                                             qe[:, (2 * j + 1) * P:(2 * j + 2) * P], start=True, stop=True)
                    else:
                        for j in range(TT):
                            t = slice(j * P, j * P + P)
                            last = pe.matmul(ps[:, bank, t], ke[:, t], qe[:, t], start=True, stop=True)
                    done(last)
                pe.wait_ge(level_merged, c.level.at(0))
                pe.wait_ge(op_ready, c.op.at(0))
                d = slice(h * P, h * P + P)
                for j in range(TT):
                    pe.matmul(ps[:, 6, j * P:j * P + P], hg_v[:, j, d], hg_s[:, j, :], start=j == 0, stop=False, skip_group_check=True)
                for j in range(2):
                    pe.matmul(ps[:, 6, (2 * j + 1) * P:(2 * j + 2) * P], hg_v[:, 2 * j, d], hg_p128[:, j, :],
                              start=False, stop=False, skip_group_check=True)
                for j in range(2):
                    last = pe.matmul(ps[:, 6, 256:512], hg_v[:, j, d], hg_p256[:, j, :], start=False, stop=j == 1, skip_group_check=True)
                last.then_inc(head_done, 1)

            pe.wait_ge(aux_evacuated, c.aux.at(0))
            pe.wait_ge(conv_ready, c.conv.at(1))
            c.conv.n += 1
            for j in range(CT):
                last = pe.matmul(ps[:, 6, :], ones_p, conv_out[:, j, :], start=j == 0, stop=j == CT - 1)
            last.then_inc(mean_done, 1)
            for g in range(4):
                gates()
                if g == 0:
                    stats(CT)
                    c.op.n += CT
                else:
                    stats(1)
                    c.op.n += 1
                if g == 0:
                    pe.wait_ge(op_ready, c.op.at(0))
                project_half(0)
                hgrn_head(g)
            stats(1)
            c.op.n += 1

            pe.wait_ge(op_ready, c.op.at(0))
            values_4(0)
            pe.wait_ge(aux_evacuated, c.aux.at(0))
            for i in range(8):
                project(bank_a())
                if i:
                    stats(1, pair_ones[:, :])
            stats(1, pair_ones[:, :])

            def sb_pair(g):
                steps = [(i, j) for i in range(2) for j in (3, 2, 1, 0)]

                def z_products(bank, i, j, stop):
                    part = slice(i * SB_DH, i * SB_DH + SB_DH)
                    return pe.matmul(ps[:, bank, 0:SB_W[j]], sb_k[part, g, j * P:j * P + P], sb_q[part, g, j * P:S], start=True, stop=stop)

                def z(i, j):
                    need(pe, sp_ready, c.z.at(-1))
                    z_products(4 + c.z.n % 2, i, j, True).then_inc(z_done, 1)
                    c.z.n += 1

                def arg(i, j):
                    pe.wait_ge(sp_ready, c.arg.at(1))
                    need(pe, a_ready, c.arg.at(-1))
                    bank = 6 + c.arg.n % 2
                    z_products(bank, i, j, False)
                    for e in range(TT - 1, j, -1):
                        pe.matmul(ps[:, bank, (e - j) * P:SB_W[j]], neg_ones[:, :], sb_sp[i][e], start=False, stop=False)
                    pe.matmul(ps[:, bank, 0:SB_W[j]], neg_tri[:, :], sb_sp[i][j], start=False, stop=True).then_inc(arg_done, 1)
                    c.arg.n += 1

                def out(bank, i):
                    part = slice(i * SB_DH, i * SB_DH + SB_DH)
                    pe.wait_ge(a_ready, c.a.at(TT))
                    c.a.n += TT
                    d = (2 * g + i) * SB_DH
                    for j in range(TT):
                        last = pe.matmul(ps[part, bank, j * P:S], sb_v[:, j, d:d + SB_DH], sb_a[i][j], start=j == 0, stop=j == TT - 1)
                    return last

                bank = None
                for n in range(10):
                    if n < 8:
                        z(*steps[n])
                    if n >= 2:
                        arg(*steps[n - 2])
                    if n == 7:
                        bank = bank_v()
                        out(bank, 0)
                tile(out(bank, 1))

            pe.wait_ge(normalised, c.rt.at(0))
            for g in range(4):
                gates()
                project_half(4)
                sb_pair(g)
            for g in range(4):
                gates()
                if g == 0:
                    pe.wait_ge(dve_evacuated, c.dve.at(0))
                project_half(0)

            for m in range(KT):
                project(bank_v(), fresh=m == 0)
            stats(KT)

            def mlp_up(fresh=False):
                project(bank_a(), fresh)
                project(bank_a())

            mlp_up(True)
            with loop(pe, MLP_CHUNKS // 2 - 1, c, units=8, tiles=20, act=4, dve=16, hid=4):
                mlp_up()
                down(0)
                mlp_up()
                down(1)
            mlp_up()
            down(0)
            down(1)

            def ffn():
                def up(fresh=False):
                    project(bank_a(), fresh)
                    project(bank_a())
                    project(bank_v())
                    project(bank_v())

                stats(KT)
                up(True)
                with loop(pe, FFN_CHUNKS // 2, c, units=12, tiles=24, act=4, dve=20, hid=4):
                    up()
                    down(0)
                    up()
                    down(1)
                down(0)

            def lru_gates(pair):
                pe.wait_ge(conv_ready, c.conv.at(1))
                need(pe, aux_evacuated, c.aux.at(0))
                pe.wait_ge(rt_ready, c.rt.at(0))
                if pair == 0:
                    pe.wait_ge(lru_loaded, c.lru.at(16))
                    c.lru.n += 16
                    pe.wait_ge(cum_ready, c.cum.at(1))
                for t in range(2):
                    for n in range(2):
                        last = pe.matmul(ps[:, 4 + 2 * t + n, :], lru_w[:, n, 2 * pair + t, :], xc[:, t, :], start=True, stop=True)
                last.then_inc(gates_done, 1)
                c.conv.n += 1
                c.aux.n += 1

            def forget_logits():
                pe.wait_ge(wf_ready, c.wf.at(1))
                c.wf.n += 1
                for t in range(TT):
                    tok = slice(t * P, t * P + P)
                    for k in range(KT):
                        out = ps[:, 4, t * HEADS:(t + 1) * HEADS]
                        pe.matmul(out, a_hi[:, k, tok], wf_lo[:, k, :], start=k == 0, stop=False)
                        pe.matmul(out, a_lo[:, k, tok], wf_hi[:, k, :], start=False, stop=False)
                        last = pe.matmul(out, a_hi[:, k, tok], wf_hi[:, k, :], start=False, stop=k == KT - 1)
                last.then_inc(f_done, 1)

            def forget_turn():
                pe.wait_ge(f_copied, c.fc.at(1))
                c.fc.n += 1
                for t in range(TT):
                    last = pe.transpose(ps[0:HEADS, 5, t * P:t * P + P], f_tok[:, t, :], ident[:, :])
                last.then_inc(f_turned, 1)

            def attend(g, steps):
                for n in steps:
                    if n < 8:
                        i, r = n // 4, n % 4
                        if c.sc.n:
                            need(pe, exp_ready, c.sc.at(-1))
                        if n == 0:
                            pe.wait_ge(cum_ready, c.cum.at(1))
                            pe.wait_ge(normalised, c.rt.at(0))
                        w = slice(0, (r + 1) * P)
                        pe.matmul(ps[:, 4 + c.sc.n % 2, w], q_h[g % 2][:, i, r * P:r * P + P], k_h[g % 2][:, i, w], start=True, stop=False)
                        h = 2 * g + i
                        pe.matmul(ps[:, 4 + c.sc.n % 2, w], ident[0:HEADS, h:h + 1].to_broadcast([HEADS, P]), neg_cum_f[:, w],
                                  start=False, stop=True).then_inc(scores_done, 1)
                        c.sc.n += 1
                    if 1 <= n <= 8:
                        r = (n - 1) % 4
                        pe.wait_ge(probs_ready, c.turn.at(1))
                        if c.turn.n:
                            need(pe, turned_copied, c.turn.at(0))
                        for j in range(r + 1):
                            last = pe.transpose(ps[:, 6, j * P:j * P + P], probs[:, c.turn.n % 2, j * P:j * P + P], ident[:, :])
                        last.then_inc(turned, 1)
                        c.turn.n += 1
                    if n in (5, 9):
                        i = n // 4 - 1
                        pe.wait_ge(turned_copied, c.pv.at(4))
                        c.pv.n += 4
                        bank = bank_v()
                        for j in range(TT):
                            last = pe.matmul(ps[:, bank, j * P:S], v_h[g % 2][:, j, i * P:i * P + P], probs_t[:, j, j * P:S],
                                             start=j == 0, stop=j == TT - 1)
                        tile(last)

            def values_2():
                pe.wait_ge(lo_ready, c.units.at(2))
                for b in range(2):
                    bank = bank_a()
                    for t in (2 * b, 2 * b + 1):
                        tok, out = slice(t * P, t * P + P), ps[:, bank, (t % 2) * 2 * P:(t % 2 + 1) * 2 * P]
                        for f in range(KT):
                            s = (c.units.n + f // 4) % RING
                            w = slice((f % 4) * 2 * P, (f % 4 + 1) * 2 * P)
                            pe.matmul(out, a_hi[:, f, tok], w_lo[:, s, w], start=f == 0, stop=False)
                            pe.matmul(out, a_lo[:, f, tok], w_hi[:, s, w], start=False, stop=False)
                            last = pe.matmul(out, a_hi[:, f, tok], w_hi[:, s, w], start=False, stop=f == KT - 1)
                    tile(last)
                c.units.n += 2

            def queries_keys_values(g, beside):
                for n in range(4):
                    project(bank_a())
                    if g == 0:
                        beside(n)
                    if n:
                        stats(1)
                    if g:
                        beside(n)
                values_2()
                stats(1)
                beside(4)

            with loop(pe, LAYERS, c, **PER_LAYER["pe"]):
                ffn()
                stats(KT)
                for j in range(4):
                    project(bank_a(), fresh=j == 0)
                    if j == 0:
                        forget_logits()
                    project(bank_a())
                    if j == 0:
                        forget_turn()
                    if j:
                        lru_gates(j - 1)
                    project(bank_a())
                    project(bank_a())

                def beside_first(n):
                    if n == 1:
                        lru_gates(3)

                queries_keys_values(0, beside_first)
                for m in range(0, KT, 2):
                    gates()
                    if m == 0:
                        c.op.n += KT
                        pe.wait_ge(op_ready, c.op.at(0))
                    project_b()
                    project_b()
                for g in range(1, 4):
                    queries_keys_values(g, lambda n: attend(g - 1, BESIDE[n]))
                for m in range(0, KT, 2):
                    project(bank_a())
                    if m == 0:
                        attend(3, range(0, 5))
                    project(bank_a())
                    if m == 0:
                        attend(3, range(5, 10))
                        c.op.n += KT
                        c.cum.n += 1
                        pe.wait_ge(op_ready, c.op.at(0))
                    project_b()
                    project_b()
                for m in range(KT):
                    project(bank_v(), fresh=m == 0)
                ffn()

        @block.scalar
        def _(act):
            c = Counts()

            def round_unit(slot, loaded):
                act.wait_ge(raw_loaded[slot], loaded)
                act.activation(w_hi[:, slot, :], raw[:, slot, :], ACT.Copy).then_inc(hi_ready, 1)

            def tick():
                need(act, tiles_done, c.tiles.at(0))
                round_unit((c.units.n + LEAD) % RING, c.units.quarter(LEAD))
                c.units.n += 1

            def evacuate(out, func, bias=0.0, scale=1.0):
                act.wait_ge(tiles_done, c.tiles.at(1))
                act.activation(out, ps[:, c.act.n % 2, :], func, bias=bias, scale=scale).then_inc(act_evacuated, 1)
                c.tiles.n += 1
                c.act.n += 1

            def pass_v(n=1):
                c.tiles.n += n
                c.dve.n += n

            def square(tile):
                need(act, stat_done, c.sq.at(-1))
                act.activation(sq[:, c.sq.n % 2, :], tile, ACT.Square).then_inc(sq_ready, 1)
                c.sq.n += 1

            def inverse_rms(n, late=0):
                act.wait_ge(stat_done, c.sq.at(-late))
                need(act, normalised, c.rt.at(0))
                act.activation(rt, ps[:, 7, :], ACT.Ln, bias=eps_col, scale=1.0 / n)
                act.drain()
                act.activation(rt, rt, ACT.Exp, scale=-0.5).then_inc(rt_ready, 1)
                c.rt.n += 1

            def round_tiles(dst, ks):
                need(act, tiles_done, c.tiles.at(0))
                for k in ks:
                    act.wait_ge(t_ready, c.t.at(1))
                    act.activation(dst[:, k, :], tt[:, c.t.n % 2, :], ACT.Copy).then_inc(op_rounded, 1)
                    c.t.n += 1

            act.wait_ge(consts_ready, 1)
            act.wait_ge(par_loaded, 16)
            act.activation(c_act, par(PAR1, "c", 0, KT), ACT.Silu).then_inc(c_ready, 1)
            act.wait_ge(keep_asked, 1)
            act.activation(keep, keep, ACT.Exp).then_inc(keep_ready, 1)
            act.wait_ge(x_loaded, 16)
            for k in range(KT):
                square(xres[:, k, :])
            inverse_rms(D)
            for u in range(LEAD):
                round_unit(u, 16)
            round_tiles(a_hi, range(KT))

            for j in range(CT):
                tick()
                pass_v()
                tick()
                need(act, dve_evacuated, c.dve.at(-2))
                evacuate(sgate[:, j % 2, :], ACT.Sigmoid)
            for h in range(HG_HEADS):
                tick()
                evacuate(hg_q[:, h, :], ACT.Silu)
            for h in range(HG_HEADS):
                tick()
                evacuate(hg_k[:, h, :], ACT.Sigmoid, scale=-1.0)

            def values_4(dst):
                for u in range(4):
                    tick()
                    c.tiles.n += 1
                act.wait_ge(tiles_done, c.tiles.at(0))
                for t in range(TT):
                    last = act.activation(dst[:, t, :], ps[:, 4 + t, :], ACT.Copy)
                last.then_inc(aux_evacuated, 1)

            values_4(hg_v)
            for h in range(HG_HEADS):
                tick()
                evacuate(hg_g[:, h, :], ACT.Silu)

            def gates(table, name, first):
                for m in range(2):
                    tick()
                    need(act, dve_evacuated, c.dve.at(0))
                    evacuate(sgate[:, m, :], ACT.Sigmoid, bias=par(table, name, first + m))

            def hgrn_head(h):
                act.wait_ge(log_asked, c.log.at(1))
                c.log.n += 1
                act.activation(hg_log, hg_log, ACT.Ln).then_inc(log_ready, 1)
                for n in range(len(LEVELS)):
                    act.wait_ge(decay_asked, c.decay.at(1))
                    c.decay.n += 1
                    act.activation(hg_e[:, n % 2, :], hg_e[:, n % 2, :], ACT.Exp).then_inc(decay_ready, 1)
                act.wait_ge(head_done, h + 1)
                square(ps[:, 6, :])

            for g in range(4):
                gates(PAR1, "gate_b", 2 * g)
                if g == 0:
                    for j in range(CT):
                        act.wait_ge(centred, j + 1)
                        square(conv_out[:, j, :])
                    inverse_rms(CONV_CH)
                    for j in range(CT):
                        act.wait_ge(t_ready, c.t.at(1))
                        t = tt[:, c.t.n % 2, :]
                        act.activation(t, t, ACT.Silu, scale=par(PAR1, "ln_g", j), bias=par(PAR1, "ln_b", j))
                        act.drain()
                        act.activation(b_hi[:, j, :], t, ACT.Copy).then_inc(op_rounded, 1)
                        c.t.n += 1
                else:
                    inverse_rms(P)
                    round_tiles(b_hi, [4 + g - 1])
                tick()
                pass_v(2)
                hgrn_head(g)
            inverse_rms(P)
            round_tiles(b_hi, [7])

            values_4(sb_v)
            for i in range(8):
                tick()
                dst = (sb_q, sb_k)[i % 2][:, i // 2, :]
                evacuate(dst, ACT.Copy)
                act.drain()
                square(dst)
                if i:
                    inverse_rms(SB_DH, 1)
            inverse_rms(SB_DH)

            def sb_pair():
                need(act, tiles_done, c.tiles.at(0))
                steps = [(i, j) for i in range(2) for j in (3, 2, 1, 0)]
                for n in range(10):
                    if n < 8:
                        i, j = steps[n]
                        b, e = c.z.n % 2, sb_e[c.z.n % 2][:, 0:SB_W[j]]
                        act.wait_ge(z_done, c.z.at(1))
                        need(act, sp_ready, c.z.at(-1))
                        act.activation(e, ps[:, 4 + b, 0:SB_W[j]], ACT.Abs)
                        act.drain()
                        act.activation(e, e, ACT.Exp, scale=-1.0)
                        act.drain()
                        act.activation(e, e, ACT.Ln, bias=one_col).then_inc(log1p_ready, 1)
                        c.z.n += 1
                    if n >= 2:
                        i, j = steps[n - 2]
                        b = c.a.n % 2
                        act.wait_ge(diag_ready, c.a.at(1))
                        if j < TT - 1:
                            act.activation(sb_a[i][j][:, P:SB_W[j]], ps[:, 6 + b, P:SB_W[j]], ACT.Exp)
                        act.activation(sb_a[i][j][:, 0:P], sb_diag[b], ACT.Exp).then_inc(a_ready, 1)
                        c.a.n += 1

            for g in range(4):
                gates(PAR1, "gate_b", KT + 2 * g)
                tick()
                pass_v(2)
                sb_pair()
                act.wait_ge(tiles_done, c.tiles.at(1))
                act.activation(b_hi[:, g, :], ps[:, 2 + c.dve.n % 2, :], ACT.Copy).then_inc(op_rounded, 1)
                pass_v()
            for g in range(4):
                gates(PAR1, "gate_b", 2 * KT + 2 * g)
                tick()
                pass_v(2)

            def round_merged(merged):
                need(act, tiles_done, c.tiles.at(0))
                for k in range(KT):
                    act.wait_ge(merged_ready, c.merged.at(1))
                    act.activation(a_hi[:, k, :], merged[:, k, :], ACT.Copy).then_inc(op_rounded, 1)
                    c.merged.n += 1

            def project_v(n):
                for m in range(n):
                    tick()
                    pass_v()

            def norm(n=KT):
                for k in range(KT):
                    act.wait_ge(dve_evacuated, c.dve.at(k + 1 - KT))
                    square(xres[:, k, :])
                inverse_rms(D)
                round_tiles(a_hi, range(KT))

            round_merged(xres)
            c.op.n += KT + 4 + HG_HEADS + KT
            act.wait_ge(op_ready, c.op.at(0))
            act.dma_start(xres[:, :, :], x_t).then_inc(x_loaded, 16)
            project_v(KT)
            norm()

            def down():
                for u in range(2):
                    tick()
                    pass_v(4)

            def mlp_up():
                for m in range(2):
                    tick()
                    need(act, hidden_ready, c.hid.at(0))
                    evacuate(sgate[:, m, :], ACT.Relu)
                c.hid.n += 2

            mlp_up()
            with loop(act, MLP_CHUNKS // 2 - 1, c, units=8, tiles=20, act=4, dve=16, hid=4):
                mlp_up()
                down()
                mlp_up()
                down()
            mlp_up()
            down()
            down()
            c.op.n += KT
            c.conv.n += 1

            def ffn():
                def up():
                    for m in range(2):
                        tick()
                        need(act, dve_evacuated, c.dve.at(0))
                        evacuate(sgate[:, m, :], ACT.Silu)
                    project_v(2)

                up()
                with loop(act, FFN_CHUNKS // 2, c, units=12, tiles=24, act=4, dve=20):
                    up()
                    down()
                    up()
                    down()
                down()

            def recurrent_gates(pair):
                act.wait_ge(gates_done, c.gates.at(1))
                c.gates.n += 1
                if pair == 0:
                    act.wait_ge(spl_ready, c.spl.at(1))
                    c.spl.n += 1
                act.wait_ge(op_ready, c.op.at(0))
                for t in range(2):
                    act.activation(rr[:, t, :], ps[:, 4 + 2 * t, :], ACT.Tanh, scale=0.5, bias=half_ba[:, 2 * pair + t:2 * pair + t + 1])
                    last = act.activation(ii[:, t, :], ps[:, 5 + 2 * t, :], ACT.Tanh, scale=0.5,
                                          bias=half_bx[:, 2 * pair + t:2 * pair + t + 1])
                last.then_inc(aux_evacuated, 1)
                act.drain()
                for t in range(2):
                    neg = tmp8[:, 2 * pair + t:2 * pair + t + 1]
                    act.activation(th[:, t, :], rr[:, t, :], ACT.Tanh, scale=neg, bias=neg)
                act.drain()
                for t in range(2):
                    pos = half_spl[:, 2 * pair + t:2 * pair + t + 1]
                    last = act.activation(rr[:, t, :], rr[:, t, :], ACT.Exp, scale=pos, bias=pos)
                last.then_inc(lru_ready, 1)

            def recurrent_root():
                act.wait_ge(root_asked, c.root.at(1))
                c.root.n += 1
                act.activation(th, th, ACT.Sqrt, scale=0.25).then_inc(root_ready, 1)

            def recurrent_out(pair):
                round_tiles(b_hi, [2 * pair, 2 * pair + 1])
                c.op.n += 2

            def attend(g, steps):
                for n in steps:
                    if n < 8:
                        b, w = c.exp.n % 2, slice(0, (n % 4 + 1) * P)
                        act.wait_ge(max_ready, c.exp.at(1))
                        if c.exp.n:
                            need(act, turned, c.exp.at(-1))
                        act.activation(probs[:, b, w], ps[:, 4 + b, w], ACT.Exp, bias=neg_max[:, b:b + 1],
                                       accum_out=den[:, b:b + 1]).then_inc(exp_ready, 1)
                        c.exp.n += 1
                    if n == 5:
                        pass_v()
                    if 1 <= n <= 8:
                        r = (n - 1) % 4
                        act.wait_ge(turned, c.turn.at(1))
                        c.turn.n += 1
                        if r == 0:
                            act.wait_ge(tiles_done, c.tiles.at(0))
                        act.activation(probs_t[:, 0:r + 1, r * P:r * P + P],
                                       ps[:, 6, 0:(r + 1) * P].rearrange("p (j t) -> p j t", t=P), ACT.Copy).then_inc(turned_copied, 1)
                    if n == 6:
                        round_tiles(b_hi, [2 * g])
                    if n == 9:
                        pass_v()
                        round_tiles(b_hi, [2 * g + 1])

            def queries_keys_values(g, beside):
                for n in range(4):
                    tick()
                    dst, name = ((q_h, "b_q"), (k_h, "b_k"))[n // 2]
                    dst = dst[g % 2][:, n % 2, :]
                    evacuate(dst, ACT.Identity, bias=par(PAR2, name, 2 * g + n % 2))
                    act.drain()
                    square(dst)
                    if g == 0:
                        beside(n)
                    if n:
                        inverse_rms(P, 1)
                    if g:
                        beside(n)
                tick()
                for b in range(2):
                    evacuate(v_h[g % 2][:, 2 * b:2 * b + 2, :].rearrange("p t d -> p (t d)"), ACT.Copy)
                tick()
                inverse_rms(P)
                beside(4)

            with loop(act, LAYERS, c, **PER_LAYER["act"]) as layer:
                act.wait_ge(dve_evacuated, c.dve.at(0))
                act.dma_start(params[:, 0:N_PAR2], par2[bass.ds(layer, 1)].rearrange("o p n -> p (o n)")).then_inc(par_loaded, 16)
                act.dma_start(arena[:, 0:2 * KT * P], lru[bass.ds(layer, 1)].rearrange("o p n -> p (o n)")).then_inc(lru_loaded, 16)
                act.wait_ge(par_loaded, c.par.at(32))
                c.par.n += 16
                act.activation(tmp8, par(PAR2, "lam", 0, KT), ACT.Abs)
                act.drain()
                act.activation(tmp8, tmp8, ACT.Exp, scale=-1.0)
                act.drain()
                act.activation(tmp8, tmp8, ACT.Ln, bias=one_col).then_inc(spl_logged, 1)
                act.activation(wf_hi[:, :, :].rearrange("p k h -> p (k h)"), par(PAR2, "w_f", 0, KT * HEADS), ACT.Copy).then_inc(wf_rounded, 1)
                norm()
                ffn()
                norm()
                for j in range(4):
                    for t in range(2):
                        tick()
                        if t == 0:
                            need(act, conv_ready, c.conv.at(0))
                        evacuate(xr[:, t, TAPS_2 - 1:TAPS_2 - 1 + S], ACT.Identity, bias=par(PAR2, "b_xr", 2 * j + t))
                    if j == 0:
                        act.wait_ge(f_asked, c.f.at(1))
                        c.f.n += 1
                        act.activation(f_abs, f_row, ACT.Abs)
                        act.drain()
                        act.activation(f_abs, f_abs, ACT.Exp, scale=-1.0)
                        act.drain()
                        act.activation(f_abs, f_abs, ACT.Ln, bias=one_col[0:HEADS, :]).then_inc(f_logged, 1)
                        c.op.n += 2 * KT
                    c.conv.n += 1
                    if j:
                        recurrent_gates(j - 1)
                    tick()
                    evacuate(gr[:, j % 2, 0, :], ACT.Gelu_apprx_tanh, bias=par(PAR2, "b_gr", 2 * j))
                    if j:
                        recurrent_root()
                    tick()
                    evacuate(gr[:, j % 2, 1, :], ACT.Gelu_apprx_tanh, bias=par(PAR2, "b_gr", 2 * j + 1))
                    if j:
                        recurrent_out(j - 1)

                def beside_first(n):
                    if n == 1:
                        recurrent_gates(3)
                    if n == 2:
                        recurrent_root()
                    if n == 3:
                        recurrent_out(3)

                queries_keys_values(0, beside_first)
                for m in range(0, KT, 2):
                    gates(PAR2, "b_gn", m)
                    project_v(2)
                for g in range(1, 4):
                    queries_keys_values(g, lambda n: attend(g - 1, BESIDE[n]))
                for m in range(0, KT, 2):
                    for t in range(2):
                        tick()
                        need(act, dve_evacuated, c.dve.at(0))
                        evacuate(sgate[:, t, :], ACT.Sigmoid, bias=par(PAR2, "b_ga", m + t))
                        if m == 0:
                            attend(3, (range(0, 5), range(5, 10))[t])
                    project_v(2)
                round_merged(merged2)
                c.op.n += 2 * KT
                project_v(KT)
                norm()
                ffn()
                c.op.n += KT

        @block.vector
        def _(dve):
            c = Counts()

            def v_tile():
                dve.wait_ge(tiles_done, c.tiles.at(1))
                c.tiles.n += 1
                c.dve.n += 1
                return ps[:, 2 + (c.dve.n - 1) % 2, :]

            def pass_a(n=1):
                c.tiles.n += n
                c.act.n += n

            def low_part(dst, src_hi, tile):
                dve.wait_ge(op_rounded, c.rounded.at(1))
                c.rounded.n += 1
                return dve.tensor_tensor(dst, tile, src_hi.bitcast(F32), ALU.subtract)

            def norm(scale, shift=None):
                dve.wait_ge(rt_ready, c.rt.at(1))
                c.rt.n += 1

                def scaled(k):
                    t = tt[:, (c.t.n + k) % 2, :]
                    ins = dve.tensor_tensor(t, xres[:, k, :], rt, ALU.mult)
                    if k == KT - 1:
                        ins.then_inc(normalised, 1)
                    dve.drain()
                    if shift is None:
                        dve.tensor_scalar(t, t, scale[:, k:k + 1], None, ALU.mult).then_inc(t_ready, 1)
                    else:
                        dve.tensor_scalar(t, t, scale[:, k:k + 1], shift[:, k:k + 1], ALU.mult, ALU.add).then_inc(t_ready, 1)
                    dve.drain()

                scaled(0)
                for k in range(KT):
                    if k + 1 < KT:
                        scaled(k + 1)
                    low_part(a_lo[:, k, :], a_hi[:, k, :], tt[:, (c.t.n + k) % 2, :]).then_inc(op_ready, 1)
                    dve.drain()
                c.t.n += KT

            dve.wait_ge(consts_ready, 1)
            dve.wait_ge(par_loaded, 16)
            lb = par(PAR1, "lb", 0, HG_HEADS)
            dve.tensor_tensor(keep, lb, lb, ALU.subtract).then_inc(keep_asked, 1)
            dve.wait_ge(keep_ready, 1)
            dve.reciprocal(tmp8[:, 0:4], keep)
            dve.drain()
            dve.tensor_tensor(keep, keep, tmp8[:, 0:4], ALU.mult)
            dve.drain()
            dve.tensor_tensor(keep, keep, keep, ALU.subtract)
            dve.drain()
            dve.tensor_scalar(keep, keep, -1.0, 1.0, ALU.mult, ALU.add)
            dve.wait_ge(mod_used, MODS)
            dve.tensor_tensor(modp, ps[:, 6, 0:MODS], par(PAR1, "mod_b", 0, MODS), ALU.add)
            dve.drain()
            for dst, at, g in ((scale1, 1, "norm1_g"), (scale2, 4, "norm2_g")):
                dve.scalar_tensor_tensor(dst, modp[:, at * KT:(at + 1) * KT], 1.0, par(PAR1, g, 0, KT), ALU.add, ALU.mult)
            dve.tensor_scalar(q_col, par(PAR1, "sbq_g"), SB_DH ** -0.5, None, ALU.mult)
            dve.memset(conv_in[:, :, 0:PAD], 0.0)
            dve.memset(hg_s, 0.0)
            dve.drain()
            norm(scale1, modp[:, 0:KT])

            for j in range(CT):
                a = v_tile()
                pass_a()
                dve.wait_ge(act_evacuated, c.act.at(0))
                dve.tensor_tensor(conv_in[:, j, PAD:PAD + S], a, sgate[:, j % 2, :], ALU.mult).then_inc(dve_evacuated, 1)
            dve.drain()
            taps = PAR1["conv_w"][0]
            for j in range(CT):
                dve.tensor_scalar(conv_out[:, j, :], conv_in[:, j, 0:S], params[:, taps + j:taps + j + 1], par(PAR1, "conv_b", j),
                                  ALU.mult, ALU.add)
            with dve.Fori(1, TAPS) as tap:
                dve.drain()
                for j in range(CT):
                    dve.scalar_tensor_tensor(conv_out[:, j, :], conv_in[:, j, bass.ds(tap, S)], params[:, bass.ds(tap * CT + (taps + j), 1)],
                                             conv_out[:, j, :], ALU.mult, ALU.add)
            dve.drain()
            dve.memset(cols[:, 126:127], 0.0).then_inc(conv_ready, 1)

            pass_a(2 * HG_HEADS)
            c.tiles.n += 4
            pass_a(HG_HEADS)
            dve.wait_ge(mean_done, 1)
            for j in range(CT):
                dve.scalar_tensor_tensor(conv_out[:, j, :], ps[:, 6, :], -1.0 / CONV_CH, conv_out[:, j, :], ALU.mult, ALU.add
                                         ).then_inc(centred, 1)
            dve.drain()
            dve.wait_ge(rt_ready, c.rt.at(1))
            c.rt.n += 1

            def ln_scaled(j):
                ins = dve.tensor_tensor(tt[:, (c.t.n + j) % 2, :], conv_out[:, j, :], rt, ALU.mult).then_inc(t_ready, 1)

            def ln_low(j):
                low_part(b_lo[:, j, :], b_hi[:, j, :], tt[:, (c.t.n + j) % 2, :]).then_inc(op_ready, 1)
                dve.drain()

            ln_scaled(0)
            ln_scaled(1)
            ln_low(0)
            ln_scaled(2)
            ln_low(1)
            ln_scaled(3)
            ln_low(2)
            ln_low(3)
            c.t.n += CT
            dve.memset(cols[:, 126:127], 0.0).then_inc(normalised, 1)

            def hgrn_head(h):
                q, k = hg_q[:, h, :], hg_k[:, h, :]
                dve.drain()
                dve.tensor_scalar(k, k, keep[:, h:h + 1], None, ALU.mult)
                dve.drain()
                dve.tensor_scalar(hg_log, k, -1.0, 1.0, ALU.mult, ALU.add).then_inc(log_asked, 1)
                dve.wait_ge(log_ready, h + 1)
                dve.tensor_tensor_scan(hg_b64, reset64, hg_log, 0.0, ALU.mult, ALU.add)
                for e in range(2):
                    part = slice(e * 256, e * 256 + 256)
                    dve.tensor_tensor_scan(hg_b256[:, part], ones[:, part], hg_log[:, part], 0.0, ALU.mult, ALU.add)
                dve.drain()

                def exponents(n):
                    m = LEVELS[n]
                    b = (hg_b256 if m >= 128 else hg_b64).rearrange("p (b h i) -> p b h i", h=2, i=m)
                    e = hg_e[:, n % 2, :].rearrange("p (b h i) -> p b h i", h=2, i=m)
                    middle = b[:, :, 0, m - 1:m].to_broadcast([P, S // (2 * m), m])
                    if m in (256, 64):
                        dve.tensor_copy(e[:, :, 1, :], b[:, :, 1, :])
                    else:
                        dve.tensor_tensor(e[:, :, 1, :], b[:, :, 1, :], middle, ALU.subtract)
                    dve.tensor_tensor(e[:, :, 0, :], middle, b[:, :, 0, :], ALU.subtract).then_inc(decay_asked, 1)

                def decayed(n):
                    dve.wait_ge(decay_ready, c.decay.at(1))
                    c.decay.n += 1
                    if n >= 2:
                        dve.wait_ge(level_done, c.level.at(n - 1))
                    dve.tensor_tensor(hg_qe[:, n % 2, :], q, hg_e[:, n % 2, :], ALU.mult)
                    dve.tensor_tensor(hg_ke[:, n % 2, :], k, hg_e[:, n % 2, :], ALU.mult).then_inc(level_ready, 1)
                    dve.drain()

                def merge(n):
                    dve.wait_ge(level_done, c.level.at(n + 1))
                    got = ps[:, 4 + (c.level.n + n) % 2, :]
                    if n == 0 and h:
                        dve.wait_ge(head_done, h)
                    if n < 2:
                        into = (hg_p256, hg_p128)[n].rearrange("p j t -> p (j t)")
                        ins = dve.tensor_copy(into, got[:, 0:(S, 2 * P)[n]])
                    else:
                        mask = masks[:, n - 2:n - 1, :].to_broadcast([P, TT, P])
                        ins = dve.copy_predicated(hg_s, mask, got.rearrange("p (j t) -> p j t", t=P))
                        dve.drain()
                    ins.then_inc(level_merged, 1)

                exponents(0)
                exponents(1)
                for n in range(len(LEVELS)):
                    decayed(n)
                    if n + 2 < len(LEVELS):
                        exponents(n + 2)
                    if n:
                        merge(n - 1)
                merge(len(LEVELS) - 1)
                merge(len(LEVELS))
                c.level.n += len(LEVELS) + 1

            def hgrn_norm(h):
                dve.wait_ge(rt_ready, c.rt.at(1))
                c.rt.n += 1
                t = tt[:, c.t.n % 2, :]
                dve.tensor_tensor(t, ps[:, 6, :], rt, ALU.mult).then_inc(normalised, 1)
                dve.drain()
                dve.scalar_tensor_tensor(t, t, par(PAR1, "hg_g"), hg_g[:, h, :], ALU.mult, ALU.mult).then_inc(t_ready, 1)
                dve.drain()
                low_part(b_lo[:, 4 + h, :], b_hi[:, 4 + h, :], t).then_inc(op_ready, 1)
                dve.drain()
                c.t.n += 1

            def gated(merged, m, first, final=False):
                y = v_tile()
                if first:
                    dve.tensor_tensor(merged[:, m, :], sgate[:, m % 2, :], y, ALU.mult).then_inc(dve_evacuated, 1)
                    return
                g = sgate[:, m % 2, :]
                dve.tensor_tensor(g, g, y, ALU.mult)
                dve.drain()
                dve.tensor_tensor(merged[:, m, :], merged[:, m, :], g, ALU.add).then_inc(dve_evacuated, 1)

            for g in range(4):
                pass_a(2)
                if g:
                    hgrn_norm(g - 1)
                hgrn_head(g)
                dve.wait_ge(act_evacuated, c.act.at(0))
                gated(xres, 2 * g, True)
                gated(xres, 2 * g + 1, True)
            hgrn_norm(3)

            c.tiles.n += 4
            for i in range(8):
                pass_a()
                dve.wait_ge(rt_ready, c.rt.at(1))
                c.rt.n += 1
                t = (sb_q, sb_k)[i % 2][:, i // 2, :]
                col = q_col if i % 2 == 0 else par(PAR1, "sbk_g")
                dve.scalar_tensor_tensor(t, t, col, rt, ALU.mult, ALU.mult).then_inc(normalised, 1)

            def sb_pair():
                steps = [(i, j) for i in range(2) for j in (3, 2, 1, 0)]
                need(dve, arg_done, c.arg.at(0))
                for n in range(10):
                    if n < 8:
                        i, j = steps[n]
                        dve.wait_ge(log1p_ready, c.z.at(1))
                        t = sb_sp[i][j]
                        ins = dve.scalar_tensor_tensor(t, ps[:, 4 + c.z.n % 2, 0:SB_W[j]], 0.0, sb_e[c.z.n % 2][:, 0:SB_W[j]], ALU.max, ALU.add)
                        dve.drain()
                        dve.tensor_tensor(t[:, 0:P], t[:, 0:P], before[:, :], ALU.mult).then_inc(sp_ready, 1)
                        c.z.n += 1
                    if n >= 2:
                        b = c.arg.n % 2
                        dve.wait_ge(arg_done, c.arg.at(1))
                        need(dve, a_ready, c.arg.at(-1))
                        dve.scalar_tensor_tensor(sb_diag[b], ps[:, 6 + b, 0:P], 0.0, hide_ge[:, :], ALU.min, ALU.add).then_inc(diag_ready, 1)
                        c.arg.n += 1

            for g in range(4):
                pass_a(2)
                dve.wait_ge(act_evacuated, c.act.at(0))
                gated(xres, 2 * g, False)
                gated(xres, 2 * g + 1, False)
                sb_pair()
                o = v_tile()
                low_part(b_lo[:, g, :], b_hi[:, g, :], o).then_inc(dve_evacuated, 1)
            for g in range(4):
                pass_a(2)
                dve.wait_ge(act_evacuated, c.act.at(0))
                gated(xres, 2 * g, False)
                gated(xres, 2 * g + 1, False)

            def split_merged(merged):
                dve.drain()
                dve.memset(cols[:, 126:127], 0.0).then_inc(merged_ready, KT)
                for k in range(KT):
                    low_part(a_lo[:, k, :], a_hi[:, k, :], merged[:, k, :]).then_inc(op_ready, 1)

            split_merged(xres)
            dve.wait_ge(x_loaded, 32)

            def add_tiles(scales):
                for m, scale in scales:
                    y = v_tile()
                    dve.scalar_tensor_tensor(xres[:, m, :], y, scale, xres[:, m, :], ALU.mult, ALU.add).then_inc(dve_evacuated, 1)

            add_tiles([(m, modp[:, 2 * KT + m:2 * KT + m + 1]) for m in range(KT)])
            dve.drain()
            norm(scale2, modp[:, 3 * KT:4 * KT])

            def hidden(half, m, t):
                n = 2 * half + m
                dve.drain()
                dve.tensor_copy(b_hi[:, n, :], t)
                dve.drain()
                dve.tensor_tensor(b_lo[:, n, :], t, b_hi[:, n, :].bitcast(F32), ALU.subtract).then_inc(hidden_ready, 1)

            def mlp_up(half):
                for m in range(2):
                    pass_a()
                    dve.wait_ge(act_evacuated, c.act.at(0))
                    t = tt[:, m, :]
                    dve.tensor_tensor(t, sgate[:, m, :], sgate[:, m, :], ALU.mult)
                    hidden(half, m, t)

            def mlp_down():
                dve.drain()
                add_tiles([(m, modp[:, 5 * KT + m:5 * KT + m + 1]) for m in range(KT)])

            mlp_up(0)
            with loop(dve, MLP_CHUNKS // 2 - 1, c, tiles=20, act=4, dve=16):
                mlp_up(1)
                mlp_down()
                mlp_up(0)
                mlp_down()
            mlp_up(1)
            mlp_down()
            mlp_down()

            def ffn():
                def up(half):
                    pass_a(2)
                    for m in range(2):
                        dve.drain()
                        y = v_tile()
                        dve.wait_ge(act_evacuated, c.act.at(0))
                        t = tt[:, m, :]
                        dve.tensor_tensor(t, sgate[:, m, :], y, ALU.mult).then_inc(dve_evacuated, 1)
                        hidden(half, m, t)

                def down():
                    dve.drain()
                    add_tiles([(m, 0.5) for m in range(KT)])

                up(0)
                with loop(dve, FFN_CHUNKS // 2, c, tiles=24, act=4, dve=20):
                    up(1)
                    down()
                    up(0)
                    down()
                down()

            def conv4(pair):
                dve.drain()
                dve.wait_ge(act_evacuated, c.act.at(0))
                for n in range(TAPS_2):
                    for t in range(2):
                        j = 2 * pair + t
                        w = par(PAR2, "conv_w", n * KT + j)
                        if n == 0:
                            ins = dve.tensor_scalar(xc[:, t, :], xr[:, t, 0:S], w, par(PAR2, "conv_b", j), ALU.mult, ALU.add)
                        else:
                            ins = dve.scalar_tensor_tensor(xc[:, t, :], xr[:, t, n:n + S], w, xc[:, t, :], ALU.mult, ALU.add)
                    if n < TAPS_2 - 1:
                        dve.drain()
                ins.then_inc(conv_ready, 1)

            def recurrence(pair):
                dve.wait_ge(lru_ready, c.lru.at(1))
                dve.scalar_tensor_tensor(ii, ii, 1.0, xc, ALU.add, ALU.mult)
                dve.drain()
                dve.tensor_tensor(xc, rr, rr, ALU.mult)
                dve.drain()
                dve.scalar_tensor_tensor(th, xc, 1.0, th, ALU.add, ALU.mult).then_inc(root_asked, 1)
                dve.wait_ge(root_ready, c.lru.at(1))
                dve.tensor_tensor(ii, ii, th, ALU.mult)
                dve.drain()
                for t in range(2):
                    dve.tensor_tensor_scan(th[:, t, :], rr[:, t, :], ii[:, t, :], 0.0, ALU.mult, ALU.add)
                dve.drain()
                dve.wait_ge(act_evacuated, c.act.at(0))
                for t in range(2):
                    dve.tensor_tensor(tt[:, t, :], th[:, t, :], gr[:, pair % 2, t, :], ALU.mult).then_inc(t_ready, 1)
                dve.drain()
                for t in range(2):
                    k = 2 * pair + t
                    low_part(b_lo[:, k, :], b_hi[:, k, :], tt[:, t, :]).then_inc(op_ready, 1)
                dve.drain()
                c.t.n += 2
                c.lru.n += 1

            def normalise(dst, col):
                dve.wait_ge(rt_ready, c.rt.at(1))
                c.rt.n += 1
                dve.scalar_tensor_tensor(dst, dst, col, rt, ALU.mult, ALU.mult).then_inc(normalised, 1)

            def attend(g, steps):
                for n in steps:
                    if n < 8:
                        r, b = n % 4, c.sc.n % 2
                        bank = ps[:, 4 + b, :]
                        dve.wait_ge(scores_done, c.sc.at(1))
                        c.sc.n += 1
                        dve.tensor_tensor(bank[:, r * P:r * P + P], bank[:, r * P:r * P + P], hide_gt[:, :], ALU.add)
                        dve.drain()
                        dve.tensor_reduce(neg_max[:, b:b + 1], bank[:, 0:(r + 1) * P], AX_X, ALU.max, negate=True).then_inc(max_ready, 1)
                    if 1 <= n <= 8:
                        r, b = (n - 1) % 4, c.pr.n % 2
                        dve.wait_ge(exp_ready, c.pr.at(1))
                        c.pr.n += 1
                        dve.reciprocal(den[:, b:b + 1], den[:, b:b + 1])
                        dve.drain()
                        p = probs[:, b, 0:(r + 1) * P]
                        dve.tensor_scalar(p, p, den[:, b:b + 1], None, ALU.mult).then_inc(probs_ready, 1)
                    if n in (5, 9):
                        h = 2 * g + n // 4 - 1
                        dve.drain()
                        o = v_tile()
                        t = tt[:, c.t.n % 2, :]
                        dve.tensor_scalar(t, o, par(PAR2, "b_v", h), None, ALU.add).then_inc(dve_evacuated, 1)
                        dve.drain()
                        dve.memset(cols[:, 126:127], 0.0).then_inc(t_ready, 1)
                        c.t.n += 1
                    if n in (6, 9):
                        h = 2 * g + (n == 9)
                        low_part(b_lo[:, h, :], b_hi[:, h, :], tt[:, (c.t.n - 1) % 2, :]).then_inc(op_ready, 1)
                        dve.drain()

            def queries_keys_values(g, beside):
                for n in range(4):
                    pass_a()
                    if n:
                        done = n - 1
                        normalise((q_h, k_h)[done // 2][g % 2][:, done % 2, :], q_col if done < 2 else par(PAR2, "k_g"))
                    beside(n)
                pass_a(2)
                normalise(k_h[g % 2][:, 1, :], par(PAR2, "k_g"))
                beside(4)

            with loop(dve, LAYERS, c, **PER_LAYER["dve"]):
                dve.wait_ge(par_loaded, c.par.at(32))
                c.par.n += 16
                dve.wait_ge(spl_logged, c.spl.at(1))
                lam = par(PAR2, "lam", 0, KT)
                dve.tensor_scalar(spl, lam, -1.0, 0.0, ALU.mult, ALU.max)
                dve.tensor_scalar(half_ba, par(PAR2, "b_a", 0, KT), 0.5, None, ALU.mult)
                dve.tensor_scalar(half_bx, par(PAR2, "b_x", 0, KT), 0.5, None, ALU.mult)
                dve.tensor_scalar(q_col, par(PAR2, "q_g"), P ** -0.5, None, ALU.mult)
                dve.drain()
                dve.tensor_tensor(spl, spl, tmp8, ALU.add)
                dve.drain()
                dve.tensor_scalar(half_spl, spl, -0.5 * LRU_C, None, ALU.mult)
                dve.tensor_scalar(tmp8, spl, 0.5 * LRU_C, None, ALU.mult).then_inc(spl_ready, 1)
                dve.wait_ge(wf_rounded, c.spl.at(1))
                c.spl.n += 1
                dve.tensor_tensor(wf_lo[:, :, :].rearrange("p k h -> p (k h)"), par(PAR2, "w_f", 0, KT * HEADS),
                                  wf_hi[:, :, :].rearrange("p k h -> p (k h)").bitcast(F32), ALU.subtract).then_inc(wf_ready, 1)
                dve.drain()
                norm(par(PAR2, "ffn1_g", 0, KT))
                ffn()
                dve.drain()
                dve.memset(xr[:, :, 0:TAPS_2 - 1], 0.0)
                norm(par(PAR2, "mix_g", 0, KT))
                for j in range(4):
                    pass_a(2)
                    if j == 0:
                        dve.wait_ge(f_done, c.cum.at(1))
                        dve.tensor_copy(f_tok.rearrange("p t h -> p (t h)"), ps[:, 4, 0:TT * HEADS]).then_inc(f_copied, 1)
                        dve.wait_ge(f_turned, c.cum.at(1))
                        dve.tensor_scalar(f_row, ps[0:HEADS, 5, :], par(PAR2, "b_f")[0:HEADS, :], None, ALU.add).then_inc(f_asked, 1)
                        dve.wait_ge(f_logged, c.cum.at(1))
                        dve.scalar_tensor_tensor(f_row, f_row, 0.0, f_abs, ALU.min, ALU.subtract)
                        dve.drain()
                        dve.tensor_scalar(f_row, f_row, -1.0, None, ALU.mult)
                        dve.drain()
                        dve.tensor_tensor_scan(neg_cum_f, ones[0:HEADS, :], f_row, 0.0, ALU.mult, ALU.add).then_inc(cum_ready, 1)
                        c.cum.n += 1
                    if j:
                        recurrence(j - 1)
                    conv4(j)
                    pass_a(2)

                def beside_first(n):
                    if n == 1:
                        recurrence(3)

                queries_keys_values(0, beside_first)
                for m in range(0, KT, 2):
                    pass_a(2)
                    dve.wait_ge(act_evacuated, c.act.at(0))
                    gated(merged2, m, True)
                    gated(merged2, m + 1, True)
                for g in range(1, 4):
                    queries_keys_values(g, lambda n: attend(g - 1, BESIDE[n]))
                for m in range(0, KT, 2):
                    pass_a()
                    if m == 0:
                        attend(3, range(0, 5))
                    pass_a()
                    if m == 0:
                        attend(3, range(5, 10))
                    dve.wait_ge(act_evacuated, c.act.at(0))
                    gated(merged2, m, False)
                    gated(merged2, m + 1, False)
                split_merged(merged2)
                dve.drain()
                add_tiles([(m, 1.0) for m in range(KT)])
                dve.drain()
                norm(par(PAR2, "ffn2_g", 0, KT))
                ffn()
            assert c.dve.at(0) == V_TILES, c.dve.n


def kernel(**inputs):
    import numpy as np
    import concourse.bacc as bacc
    from concourse.bass_utils import run_bass_kernel_spmd as run

    a = {k: np.asarray(v) for k, v in inputs.items()}

    def tall(v):
        return np.ascontiguousarray(np.reshape(v, (-1, P)).T)

    def units(w):
        return w.reshape(KT, P, -1, P).transpose(2, 1, 0, 3).reshape(-1, P, D)

    def halves(w):
        return w.reshape(4, P, 4, 2 * P).transpose(2, 1, 0, 3).reshape(4, P, D)

    def moving(w):
        rows = D // w.shape[1]
        return w.reshape(KT // rows, rows, P, -1).transpose(0, 2, 1, 3).reshape(-1, P, D)

    def downs(w):
        return w.reshape(-1, 2, P, 2, 4 * P).transpose(0, 3, 2, 1, 4).reshape(-1, 2, P, D)

    def weave(*parts):
        n = len(parts[0][0]) // parts[0][1]
        return [u for i in range(n) for w, k in parts for u in w[i * k:i * k + k]]

    def chunks(ups, down):
        out = list(ups[0])
        for i in range(1, len(ups)):
            out += list(ups[i]) + list(down[i - 1])
        return out + list(down[-1])

    w = a["w_in"][0]
    cut = lambda at, n: w[:, at:at + n]
    w1, w2 = units(a["mlp_w1"][0]), downs(a["mlp_w2"][0])
    gate = units(cut(4608, 3 * D))
    order = weave((units(cut(0, 512)), 1), (units(cut(512, 512)), 1))
    order += list(units(cut(1024, 1024))) + list(moving(cut(2048, 512))) + list(units(cut(2560, 512)))
    order += weave((gate[0:8], 2), (halves(a["w_conv_proj"][0]), 1))
    order += list(moving(cut(4096, 512))) + weave((units(cut(3072, 512)), 1), (units(cut(3584, 512)), 1))
    order += weave((gate[8:16], 2), (halves(a["w_hgrn_proj"][0]), 1))
    order += weave((gate[16:24], 2), (halves(a["w_sb_proj"][0]), 1))
    order += list(units(a["w_out"][0]))
    order += chunks([w1[2 * i:2 * i + 2] for i in range(MLP_CHUNKS)], w2)

    lru, par2 = [], []
    for l in range(LAYERS):
        def ffn(n):
            g, u = units(a[f"ffn{n}_w_gate_2"][l]), units(a[f"ffn{n}_w_up_2"][l])
            return chunks([list(g[2 * i:2 * i + 2]) + list(u[2 * i:2 * i + 2]) for i in range(FFN_CHUNKS)], downs(a[f"ffn{n}_w_down_2"][l]))

        w, b = a["w_in_2"][l], a["b_in_2"][l]
        at = 3 * D + HEADS
        order += ffn(1)
        order += weave((units(cut(at, D)), 2), (units(cut(at + D, D)), 2))
        qkv = [list(units(cut(2 * P * g, 2 * P))) + list(units(cut(D + 2 * P * g, 2 * P))) + list(moving(cut(2 * D + 2 * P * g, 2 * P)))
               for g in range(4)]
        order += qkv[0] + weave((units(cut(at + 3 * D, D)), 2), (units(a["w_o_rnn_2"][l]), 2)) + qkv[1] + qkv[2] + qkv[3]
        order += weave((units(cut(at + 2 * D, D)), 2), (units(a["w_o_attn_2"][l]), 2))
        order += list(units(a["w_out_2"][l]))
        order += ffn(2)

        block = np.zeros((P, 2, KT, P), np.float32)
        for n, name in enumerate(("lru_w_a_2", "lru_w_x_2")):
            pairs = a[name][l].reshape(KT, 2, 64, 64)
            block[0:64, n, :, 0:64] = pairs[:, 0].transpose(1, 0, 2)
            block[64:128, n, :, 64:128] = pairs[:, 1].transpose(1, 0, 2)
        lru.append(block.reshape(P, -1))
        b_f = np.zeros((P, 1), np.float32)
        b_f[0:HEADS, 0] = b[3 * D:at]
        par2.append(np.concatenate([
            tall(a["ffn1_norm_2"][l]), tall(a["mix_norm_2"][l]), tall(a["ffn2_norm_2"][l]), tall(b[0:D]), tall(b[D:2 * D]),
            tall(b[2 * D:3 * D]), b_f, tall(b[at:at + D]), tall(b[at + D:at + 2 * D]), tall(b[at + 2 * D:at + 3 * D]),
            tall(b[at + 3 * D:at + 4 * D]), tall(a["q_norm_2"][l]), tall(a["k_norm_2"][l]), tall(a["conv_w_2"][l]),
            tall(a["conv_b_2"][l]), tall(a["lru_b_a_2"][l]), tall(a["lru_b_x_2"][l]), tall(a["lru_lambda_2"][l]),
            w[:, 3 * D:at].reshape(KT, P, HEADS).transpose(1, 0, 2).reshape(P, -1)], axis=1))
    assert len(order) == UNITS
    order += [np.zeros((P, D), np.float32)] * RING

    twice = lambda v: np.concatenate([v, v], axis=1)
    par1 = np.concatenate([
        tall(a["c"]), tall(a["mod_b"]), tall(a["norm1_g"]), tall(a["gate_b"]), tall(a["conv_w"]), tall(a["conv_b"]), tall(a["conv_ln_g"]),
        tall(a["conv_ln_b"]), tall(a["hgrn_lb"]), tall(a["hgrn_norm_g"]), tall(twice(a["sb_qn_g"])), tall(twice(a["sb_kn_g"])),
        tall(a["norm2_g"])], axis=1)
    arrays = {
        "x_t": np.ascontiguousarray(a["x"][0].T.reshape(KT, P, S).transpose(1, 0, 2)),
        "par1": np.ascontiguousarray(par1),
        "par2": np.ascontiguousarray(np.stack(par2)),
        "lru": np.ascontiguousarray(np.stack(lru)),
        "mod_w": np.ascontiguousarray(units(a["mod_w"][0])),
        "stream": np.ascontiguousarray(np.stack(order)),
    }
    nc = bacc.Bacc("TRN2", target_bir_lowering=False, num_devices=1, dynamic_dma_scratch_size=1024)
    args = [nc.dram_tensor(f"in_{n}", v.shape, F32, kind="ExternalInput").ap() for n, v in arrays.items()]
    out = nc.dram_tensor("out_t", (P, KT, S), F32, kind="ExternalOutput").ap()
    build(nc, *args, out)
    r = run(nc, [{f"in_{n}": v for n, v in arrays.items()}], core_ids=[0])
    return np.ascontiguousarray(r.results[0]["out_t"].transpose(2, 1, 0).reshape(1, S, D))
```

```python
from contextlib import ExitStack, contextmanager

import concourse.bass as bass
from concourse import mybir

F32 = mybir.dt.float32
F32R = mybir.dt.float32r
I8 = mybir.dt.int8
ALU = mybir.AluOpType
ACT = mybir.ActivationFunctionType
AX_X = mybir.AxisListType.X

P = 128
S = 512
D = 1024
KT = D // P
TT = S // P
RING = 3
WIDE = 4
MODS = 6 * KT
MOD_RING = 8
CONV_CH = 512
CT = CONV_CH // P
TAPS = 31
PAD = TAPS - 1
HG_HEADS = 4
SB_HEADS = 8
SB_DH = 64
MLP_CHUNKS = 4 * D // (2 * P)
LAYERS = 2
HEADS = 8
TAPS_2 = 4
FFN_CHUNKS = 2816 // (2 * P)
LRU_C = 8.0
EPS = 1e-6
NEG = -1e30
LEVELS = (256, 128, 64, 32, 16, 8, 4, 2, 1)
STEPS = 8 + 3
V_TILES = (4 + 4 * 2 * 3 + 4 + 8 + 8 * MLP_CHUNKS) + LAYERS * (2 * 10 * FFN_CHUNKS + 8 + 8 + 8 + 8)
PER_LAYER = {"pe": {"act": 100, "aux": 4, "conv": 4, "cum": 1, "dve": 252, "hid": 44, "lru": 16, "op": 48, "pv": 32, "rt": 19, "sc": 32, "singles": 16, "sq": 22, "sums": 18, "squares": 24, "tiles": 353, "turn": 32, "units": 213}, "act": {"act": 100, "conv": 4, "dve": 252, "exp": 32, "f": 1, "gates": 4, "merged": 8, "op": 48, "par": 16, "root": 4, "rt": 19, "spl": 1, "sq": 22, "sums": 18, "t": 40, "tiles": 353, "turn": 32, "units": 213}, "dve": {"act": 100, "cum": 1, "dve": 252, "lru": 4, "par": 16, "pr": 32, "rounded": 48, "rt": 19, "sc": 32, "spl": 1, "squares": 24, "t": 40, "tiles": 353}}
UNITS = (60 + 12 + 8 + 64) + LAYERS * (2 * 66 + 1 + 16 + 24 + 16 + 16 + 8)
LEAD = 2

PAR1 = {}
for _name, _n in (("mod_b", MODS), ("norm1_g", KT), ("gate_b", 3 * KT), ("conv_w", TAPS * CT), ("conv_b", CT),
                  ("ln_g", CT), ("ln_b", CT), ("lb", HG_HEADS), ("hg_g", 1), ("sbq_g", 1), ("sbk_g", 1), ("norm2_g", KT)):
    PAR1[_name] = (sum(n for _, n in PAR1.values()), _n)
N_PAR1 = sum(n for _, n in PAR1.values())
PAR2 = {}
for _name, _n in (("ffn1_g", KT), ("mix_g", KT), ("ffn2_g", KT), ("b_q", KT), ("b_k", KT), ("b_v", KT), ("b_f", 1), ("b_xr", KT),
                  ("b_gr", KT), ("b_ga", KT), ("b_gn", KT), ("q_g", 1), ("k_g", 1), ("conv_w", TAPS_2 * KT), ("conv_b", KT),
                  ("b_a", KT), ("b_x", KT), ("lam", KT)):
    PAR2[_name] = (sum(n for _, n in PAR2.values()), _n)
N_PAR2 = sum(n for _, n in PAR2.values())


class Count:

    def __init__(self):
        self.n = 0
        self.turns = []
        self.ring = 2

    def at(self, more=0):
        value = self.n + more
        for register, per in self.turns:
            value = register * per + value
        return value

    def quarter(self, more):
        value = 16 * ((self.n + more) // RING + 1)
        for register, per in self.turns:
            value = register * (16 * per // RING) + value
        return value


class Counts:

    def __init__(self):
        self.a = Count()
        self.act = Count()
        self.arg = Count()
        self.aux = Count()
        self.conv = Count()
        self.cum = Count()
        self.decay = Count()
        self.dve = Count()
        self.exp = Count()
        self.f = Count()
        self.fc = Count()
        self.gates = Count()
        self.hid = Count()
        self.level = Count()
        self.log = Count()
        self.lru = Count()
        self.merged = Count()
        self.mod = Count()
        self.op = Count()
        self.par = Count()
        self.pr = Count()
        self.pv = Count()
        self.ready = Count()
        self.root = Count()
        self.rounded = Count()
        self.rt = Count()
        self.sc = Count()
        self.spl = Count()
        self.sums = Count()
        self.squares = Count()
        self.singles = Count()
        self.sq = Count()
        self.t = Count()
        self.tiles = Count()
        self.turn = Count()
        self.units = Count()
        self.wf = Count()
        self.z = Count()
        self.named = {"a": self.a, "act": self.act, "arg": self.arg, "aux": self.aux, "conv": self.conv, "cum": self.cum,
                      "decay": self.decay, "dve": self.dve, "exp": self.exp, "f": self.f, "fc": self.fc, "gates": self.gates, "hid":
                      self.hid, "level": self.level, "log": self.log, "lru": self.lru, "merged": self.merged, "mod": self.mod, "op":
                      self.op, "par": self.par, "pr": self.pr, "pv": self.pv, "ready": self.ready, "root": self.root, "rounded":
                      self.rounded, "rt": self.rt, "sc": self.sc, "spl": self.spl, "singles": self.singles, "sq": self.sq, "sums": self.sums, "squares": self.squares, "t": self.t, "tiles": self.tiles, "turn":
                      self.turn, "units": self.units, "wf": self.wf, "z": self.z}




@contextmanager
def loop(eng, trips, counts, **per):
    before = {k: v.n for k, v in counts.named.items()}
    with eng.Fori(0, trips) as i:
        for name, n in per.items():
            counts.named[name].turns.append((i, n))
        yield i
        went = {k: v.n - before.get(k, 0) for k, v in counts.named.items() if v.n != before.get(k, 0)}
        assert went == {k: n for k, n in per.items() if n}, went
        for name in per:
            counts.named[name].turns.pop()
    for name, n in per.items():
        counts.named[name].n += (trips - 1) * n


def need(eng, sem, value):
    if not isinstance(value, int) or value > 0:
        eng.wait_ge(sem, value)


def build(nc, x_t, c_row, par1, par2, lru, mod_w, stream, out_t):
    with ExitStack() as ctx:
        def sb(name, shape, dt=F32):
            return ctx.enter_context(nc.sbuf_tensor(name, shape, dt))

        def sem(name):
            return ctx.enter_context(nc.semaphore(name))

        ps = ctx.enter_context(nc.psum_tensor("ps", [P, 8, S], F32))
        raw = sb("raw", [P, RING, D])
        w_hi = sb("w_hi", [P, RING, D], F32R)
        w_lo = sb("w_lo", [P, RING, D], F32R)
        a_hi, a_lo = sb("a_hi", [P, KT, S], F32R), sb("a_lo", [P, KT, S], F32R)
        b_hi, b_lo = sb("b_hi", [P, KT, S], F32R), sb("b_lo", [P, KT, S], F32R)
        xres = sb("xres", [P, KT, S])
        params = sb("params", [P, max(N_PAR1, N_PAR2)])
        cols = sb("cols", [P, 128])
        ident = sb("ident", [P, P])
        ones = sb("ones", [P, S])
        pair_ones = sb("pair_ones", [P, P])
        neg_tri = sb("neg_tri", [P, P])
        before = sb("before", [P, P])
        hide_ge = sb("hide_ge", [P, P])
        hide_gt = sb("hide_gt", [P, P])
        masks = sb("masks", [P, 8, P], I8)
        sgate = sb("sgate", [P, 2, S])
        row_tile = sb("row_tile", [P, S])
        BRANCH = 12 * S
        ARENA = 17016 + BRANCH
        arena = sb("arena", [P, ARENA])

        def area(at, *dims):
            n = 1
            for d in dims:
                n *= d
            assert at + n <= ARENA
            flat = arena[:, at:at + n]
            if len(dims) == 1:
                return flat
            names = "abc"[:len(dims)]
            return flat.rearrange(f"p ({' '.join(names)}) -> p {' '.join(names)}", **dict(zip(names, dims)))

        def par(table, name, i=0, n=1):
            at, size = table[name]
            assert i + n <= size
            return params[:, at + i:at + i + n]

        modp = cols[:, 8:56]
        scale1 = cols[:, 56:64]
        scale2 = cols[:, 64:72]
        keep = cols[:, 72:76]
        q_col = cols[:, 76:77]
        eps_col = cols[:, 77:78]
        one_col = cols[:, 78:79]
        spl = cols[:, 80:88]
        half_spl = cols[:, 88:96]
        half_ba = cols[:, 96:104]
        half_bx = cols[:, 104:112]
        tmp8 = cols[:, 112:120]
        ones_p = ones[:, 0:P]

        N0 = ARENA - BRANCH - 6 * S
        sq, rt, tt, sq_sum = area(N0, 2, S), area(N0 + 2 * S, S), area(N0 + 3 * S, 2, S), area(N0 + 5 * S, S)

        U0, C0 = 0, CT * (PAD + S)
        D0 = C0 + CT * S
        Q0 = D0 + 16 * S
        assert Q0 + 3 * S <= N0
        conv_in, conv_out = area(U0, CT, PAD + S), area(C0, CT, S)
        hg_q, hg_k, hg_v, hg_g = (area(D0 + i * 4 * S, 4, S) for i in range(4))
        mod_stage, c_act = area(U0, MOD_RING, D), area(U0 + MOD_RING * D, D)
        hg_b64, hg_b256 = area(0, S), area(S, S)
        hg_e, hg_qe, hg_ke = area(2 * S, 2, S), area(4 * S, 2, S), area(6 * S, 2, S)
        hg_log = hg_qe[:, 1, :]
        assert 8 * S <= D0
        hg_s, hg_p256, hg_p128 = area(Q0, TT, P), area(Q0 + S, 2, 256), area(Q0 + 2 * S, 2, P)
        sb_q, sb_k, sb_v = (area(ARENA - BRANCH + i * 4 * S, 4, S) for i in range(3))

        def sb_gate(m):
            return (hg_q, hg_v)[m // 4][:, m % 4, :]

        SB_W = [S - P * j for j in range(TT)]
        SB_AT = [sum(SB_W[:j]) for j in range(TT)]
        sb_a = [[area(i * sum(SB_W) + SB_AT[j], SB_W[j]) for j in range(TT)] for i in range(2)]
        sb_sp = [[area(D0 + (1 + 2 * i) * 4 * S + SB_AT[j], SB_W[j]) for j in range(TT)] for i in range(2)]
        sb_e = [area(2 * sum(SB_W) + i * S, S) for i in range(2)]
        sb_diag = [area(2 * sum(SB_W) + 2 * S + i * P, P) for i in range(2)]
        assert 2 * sum(SB_W) + 2 * S + 2 * P <= D0
        reset64 = row_tile[:, :]

        R0 = 4 * S
        lru_w = area(0, 2, KT, P)
        XW = TAPS_2 - 1 + S + 1
        xr = area(R0, 2, XW)
        gr = area(R0 + 2 * XW, 2, 2, S)
        RT = R0 + 2 * XW + 4 * S
        xc, rr, ii, th = (area(RT + i * 2 * S, 2, S) for i in range(4))
        QKV = 6 * S
        merged2 = area(R0, KT, S)
        qkv_at = [RT + 8 * S, R0 + KT * S]
        assert qkv_at[1] + QKV <= qkv_at[0]
        q_h = [area(at, 2, S) for at in qkv_at]
        k_h = [area(at + 2 * S, 2, S) for at in qkv_at]
        v_h = [area(at + 4 * S, TT, 2 * P) for at in qkv_at]
        T0 = qkv_at[0] + QKV
        def attn_gate(m):
            return area(qkv_at[0] + m * S, S) if m < QKV // S else sgate[:, m - QKV // S, :]

        probs = area(T0, 2, S)
        probs_t = area(0, TT, S)
        neg_max, den = area(T0 + 2 * S + 32, 2), area(T0 + 2 * S + 34, 2)
        assert T0 + 2 * S + 64 <= N0
        neg_cum_f = row_tile[0:HEADS, :]
        f_row, f_abs = tt[0:HEADS, 0, :], tt[0:HEADS, 1, :]

        c_loaded, par_loaded, x_loaded, lru_loaded, out_stored = sem("c_loaded"), sem("par_loaded"), sem("x_loaded"), sem("lru_loaded"), sem("out_stored")
        mod_loaded = [sem(f"mod_loaded{i}") for i in range(MOD_RING)]
        raw_loaded = [sem(f"raw_loaded{i}") for i in range(RING)]
        mod_used, mod_ready, c_ready, consts_ready = sem("mod_used"), sem("mod_ready"), sem("c_ready"), sem("consts_ready")
        hi_ready, lo_ready = sem("hi_ready"), sem("lo_ready")
        tiles_done, act_evacuated, dve_evacuated, aux_evacuated = (
            sem("tiles_done"), sem("act_evacuated"), sem("dve_evacuated"), sem("aux_evacuated"))
        sq_ready, x_sq_ready, x_sq_added = sem("sq_ready"), sem("x_sq_ready"), sem("x_sq_added")
        stat_done, rt_ready, normalised = sem("stat_done"), sem("rt_ready"), sem("normalised")
        t_ready, op_rounded, op_ready, hidden_ready = sem("t_ready"), sem("op_rounded"), sem("op_ready"), sem("hidden_ready")
        conv_ready, mean_done, centred, merged_ready = sem("conv_ready"), sem("mean_done"), sem("centred"), sem("merged_ready")
        keep_asked, keep_ready, log_asked, log_ready = sem("keep_asked"), sem("keep_ready"), sem("log_asked"), sem("log_ready")
        decay_asked, decay_ready, level_ready, level_done, level_merged, head_done = (
            sem("decay_asked"), sem("decay_ready"), sem("level_ready"), sem("level_done"), sem("level_merged"), sem("head_done"))
        z_done, neg_abs_ready, log1p_ready, sp_ready, arg_done, diag_ready, a_ready, sigmoid_ready = (
            sem("z_done"), sem("neg_abs_ready"), sem("log1p_ready"), sem("sp_ready"), sem("arg_done"), sem("diag_ready"), sem("a_ready"),
            sem("sigmoid_ready"))
        spl_logged, spl_ready = (
            sem("spl_logged"), sem("spl_ready"))
        f_asked, f_logged, cum_ready = (
            sem("f_asked"), sem("f_logged"), sem("cum_ready"))
        gates_done, lru_ready, root_asked, root_ready = sem("gates_done"), sem("lru_ready"), sem("root_asked"), sem("root_ready")
        scores_done, max_ready, exp_ready, probs_ready, turned, turned_copied = (
            sem("scores_done"), sem("max_ready"), sem("exp_ready"), sem("probs_ready"), sem("turned"), sem("turned_copied"))

        block = ctx.enter_context(nc.Block())

        @block.sync
        def _(sp):
            sp.dma_start(params[:, 0:N_PAR1], par1).then_inc(par_loaded, 16)
            sp.dma_start(xres[:, :, :], x_t).then_inc(x_loaded, 16)
            sp.dma_start(c_act, c_row.to_broadcast([P, D])).then_inc(c_loaded, 16)
            for s in range(MOD_RING):
                sp.dma_start(mod_stage[:, s, :], mod_w[s]).then_inc(mod_loaded[s], 16)
            with sp.Fori(1, MODS // MOD_RING) as i:
                for s in range(MOD_RING):
                    sp.wait_ge(mod_used, i * MOD_RING + (s + 1 - MOD_RING))
                    sp.dma_start(mod_stage[:, s, :], mod_w[bass.ds(i * MOD_RING + s, 1)].rearrange("o p n -> p (o n)")
                                 ).then_inc(mod_loaded[s], 16)
            for s in range(RING):
                sp.dma_start(raw[:, s, :], stream[s]).then_inc(raw_loaded[s], 16)
            with sp.Fori(1, UNITS // RING + 1) as i:
                for s in range(RING):
                    sp.wait_ge(lo_ready, i * RING + (s + 1 - RING))
                    sp.dma_start(raw[:, s, :], stream[bass.ds(i * RING + s, 1)].rearrange("o p n -> p (o n)")
                                 ).then_inc(raw_loaded[s], 16)
            sp.wait_ge(dve_evacuated, V_TILES)
            sp.dma_start(out_t, xres[:, :, :]).then_inc(out_stored, 16)
            for s in range(RING):
                sp.wait_ge(raw_loaded[s], 16 * (UNITS // RING + 1))
            sp.wait_ge(out_stored, 16)

        @block.gpsimd
        def _(pool):
            pool.memset(ones[:, :], 1.0)
            pool.memset(neg_tri[:, :], -1.0)
            pool.memset(before[:, :], 1.0)
            for t in (ident, hide_ge, hide_gt, pair_ones):
                pool.memset(t[:, :], 0.0)
            pool.memset(masks[:, :, :], 0)
            pool.memset(reset64, 1.0)
            pool.memset(cols[:, :], 0.0)
            pool.drain()
            pool.memset(eps_col, EPS)
            pool.memset(one_col, 1.0)
            pool.memset(reset64.rearrange("p (c t) -> p c t", t=64)[:, :, 0:1], 0.0)
            pool.drain()
            pool.memset(pair_ones[0:64, 0:64], 1.0)
            pool.drain()
            pool.memset(pair_ones[64:128, 64:128], 1.0)
            pool.drain()
            pool.affine_select(out=ident[:, :], in_=ident[:, :], compare_op=ALU.not_equal, fill=1.0, base=0,
                               pattern=[[-1, P]], channel_multiplier=1)
            pool.affine_select(out=neg_tri[:, :], in_=neg_tri[:, :], compare_op=ALU.is_ge, fill=0.0, base=0,
                               pattern=[[-1, P]], channel_multiplier=1)
            pool.affine_select(out=hide_gt[:, :], in_=hide_gt[:, :], compare_op=ALU.is_ge, fill=NEG, base=0,
                               pattern=[[-1, P]], channel_multiplier=1)
            pool.affine_select(out=before[:, :], in_=before[:, :], compare_op=ALU.is_gt, fill=0.0, base=0,
                               pattern=[[1, P]], channel_multiplier=-1)
            pool.affine_select(out=hide_ge[:, :], in_=hide_ge[:, :], compare_op=ALU.is_gt, fill=NEG, base=0,
                               pattern=[[1, P]], channel_multiplier=-1)
            pool.affine_select(out=masks[:, 7, :], in_=masks[:, 7, :], compare_op=ALU.not_equal, fill=1.0, base=0,
                               pattern=[[-1, P]], channel_multiplier=1)
            halves = [(m, masks[:, n, :].rearrange("p (b h i) -> p b h i", h=2, i=m)[:, :, 1, :]) for n, m in enumerate(LEVELS[2:])]
            for m, second in halves:
                pool.memset(second, 1)
            pool.drain()
            for m, second in halves:
                pool.affine_select(out=second, in_=second, compare_op=ALU.is_ge, fill=0.0, base=0,
                                   pattern=[[-2 * m, P // (2 * m)], [0, m]], channel_multiplier=1)
            pool.drain()
            for m, second in halves:
                pool.affine_select(out=second, in_=second, compare_op=ALU.is_ge, fill=0.0, base=m - 1,
                                   pattern=[[2 * m, P // (2 * m)], [0, m]], channel_multiplier=-1)
            pool.drain()
            pool.memset(cols[:, 127:128], 0.0).then_inc(consts_ready, 1)
            with pool.Fori(0, UNITS // RING) as i:
                for s in range(RING):
                    pool.wait_ge(hi_ready, i * RING + (s + 1))
                    pool.tensor_tensor(w_lo[:, s, :], raw[:, s, :], w_hi[:, s, :].bitcast(F32), ALU.subtract).then_inc(lo_ready, 1)

        @block.tensor
        def _(pe):
            c = Counts()

            def mm3(out, hi, lo, x_hi, x_lo, start, stop):
                pe.matmul(out, lo, x_hi, start=start, stop=False)
                pe.matmul(out, hi, x_lo, start=False, stop=False)
                return pe.matmul(out, hi, x_hi, start=False, stop=stop)

            def unit():
                pe.wait_ge(lo_ready, c.units.at(1))
                c.units.n += 1
                return (c.units.n - 1) % RING

            def bank_a():
                need(pe, act_evacuated, c.act.at(-1))
                c.act.n += 1
                return (c.act.n - 1) % 2

            def bank_v():
                need(pe, dve_evacuated, c.dve.at(1 - c.dve.ring))
                c.dve.n += 1
                return 2 + (c.dve.n - 1) % c.dve.ring

            def tile(last):
                last.then_inc(tiles_done, 1)
                c.tiles.n += 1

            def project(bank, between=None):
                s = unit()
                for k in range(KT):
                    if between and k == KT // 2:
                        between()
                    w = slice(k * P, k * P + P)
                    last = mm3(ps[:, bank, :], w_hi[:, s, w], w_lo[:, s, w], a_hi[:, k, :], a_lo[:, k, :], k == 0, k == KT - 1)
                tile(last)

            def project_fresh(*banks):
                slots = [unit(), unit()]
                for k in range(KT):
                    pe.wait_ge(op_ready, c.op.at(k + 1))
                    w = slice(k * P, k * P + P)
                    last = [mm3(ps[:, bank, :], w_hi[:, s, w], w_lo[:, s, w], a_hi[:, k, :], a_lo[:, k, :], k == 0, k == KT - 1)
                            for s, bank in zip(slots, banks)]
                c.op.n += KT
                tile(last[0])
                tile(last[1])

            def project_half(first):
                s = unit()
                for m in range(2):
                    bank = bank_v()
                    for k in range(4):
                        w = slice(k * 2 * P + m * P, k * 2 * P + m * P + P)
                        last = mm3(ps[:, bank, :], w_hi[:, s, w], w_lo[:, s, w], b_hi[:, first + k, :], b_lo[:, first + k, :],
                                   k == 0, k == 3)
                    tile(last)

            def project_b():
                s = unit()
                bank = bank_v()
                for k in range(KT):
                    w = slice(k * P, k * P + P)
                    last = mm3(ps[:, bank, :], w_hi[:, s, w], w_lo[:, s, w], b_hi[:, k, :], b_lo[:, k, :], k == 0, k == KT - 1)
                tile(last)

            def down(part):
                pe.wait_ge(hidden_ready, c.hid.at(2))
                c.hid.n += 2
                for _ in range(2):
                    s = unit()
                    for m in range(4):
                        bank = bank_v()
                        for k in range(2):
                            w = slice(k * 4 * P + m * P, k * 4 * P + m * P + P)
                            last = mm3(ps[:, bank, :], w_hi[:, s, w], w_lo[:, s, w], b_hi[:, 2 * part + k, :], b_lo[:, 2 * part + k, :],
                                       k == 0, k == 1)
                        tile(last)

            def stats(n, weights=ones_p):
                need(pe, rt_ready, c.rt.at(0))
                need(pe, aux_evacuated, c.aux.at(0))
                for k in range(n):
                    pe.wait_ge(sq_ready, c.singles.at(1))
                    c.singles.n += 1
                    pe.matmul(ps[:, 7, :], weights, sq[:, c.sq.n % 2, :], start=k == 0, stop=k == n - 1).then_inc(stat_done, 1)
                    c.sq.n += 1
                c.rt.n += 1

            def x_stats():
                need(pe, rt_ready, c.rt.at(0))
                need(pe, aux_evacuated, c.aux.at(0))
                pe.wait_ge(x_sq_added, c.sums.at(KT - 2))
                pe.matmul(ps[:, 7, :], ones_p, sq_sum, start=True, stop=False).then_inc(stat_done, 1)
                pe.wait_ge(x_sq_ready, c.squares.at(KT))
                pe.matmul(ps[:, 7, :], ones_p, sq[:, (KT - 1) % 2, :], start=False, stop=True).then_inc(stat_done, 1)
                c.sums.n += KT - 2
                c.squares.n += KT
                c.sq.n += 2
                c.rt.n += 1

            def values_4(first):
                need(pe, aux_evacuated, c.aux.at(0))
                for u in range(4):
                    s = unit()
                    for t in range(TT):
                        for k in range(2):
                            w, f, tok = slice(k * S, k * S + S), 2 * u + k, slice(t * P, t * P + P)
                            start, stop = u == 0 and k == 0, u == 3 and k == 1
                            pe.matmul(ps[:, 4 + t, :], a_hi[:, f, tok], w_lo[:, s, w], start=start, stop=False)
                            pe.matmul(ps[:, 4 + t, :], a_lo[:, f, tok], w_hi[:, s, w], start=False, stop=False)
                            last = pe.matmul(ps[:, 4 + t, :], a_hi[:, f, tok], w_hi[:, s, w], start=False, stop=stop)
                    tile(last)
                c.aux.n += 1

            def values_2(between):
                pe.wait_ge(lo_ready, c.units.at(2))
                bank = None
                for t in range(TT):
                    if t % 2 == 0:
                        bank = bank_a()
                    tok, out = slice(t * P, t * P + P), ps[:, bank, (t % 2) * 2 * P:(t % 2 + 1) * 2 * P]
                    for f in range(KT):
                        s = (c.units.n + f // 4) % RING
                        w = slice((f % 4) * 2 * P, (f % 4 + 1) * 2 * P)
                        pe.matmul(out, a_hi[:, f, tok], w_lo[:, s, w], start=f == 0, stop=False)
                        pe.matmul(out, a_lo[:, f, tok], w_hi[:, s, w], start=False, stop=False)
                        last = pe.matmul(out, a_hi[:, f, tok], w_hi[:, s, w], start=False, stop=f == KT - 1)
                    if t % 2:
                        tile(last)
                    between(t)
                c.units.n += 2

            pe.wait_ge(consts_ready, 1)
            x_stats()

            project_fresh(bank_v(), bank_a())
            for j in range(1, CT):
                project(bank_v())
                project(bank_a())
            for h in range(2 * HG_HEADS):
                project(bank_a())
            values_4(0)
            for h in range(HG_HEADS):
                project(bank_a())

            def gates():
                project(bank_a())
                project(bank_a())

            def hgrn_level(h, n):
                m = (LEVELS + (0,))[n]
                bank = 4 + c.level.n % 2
                if m:
                    pe.wait_ge(level_ready, c.ready.at(1))
                    c.ready.n += 1
                need(pe, level_merged, c.level.at(-1))
                ke, qe = (hg_ke[:, n % 2, :], hg_qe[:, n % 2, :]) if m else (hg_k[:, h, :], hg_q[:, h, :])
                if m == 256:
                    for j in range(2):
                        last = pe.matmul(ps[:, bank, j * 256:j * 256 + 256], ke[:, j * P:j * P + P], qe[:, 256:512], start=True, stop=True)
                elif m == 128:
                    for j in range(2):
                        last = pe.matmul(ps[:, bank, j * P:j * P + P], ke[:, 2 * j * P:2 * j * P + P],
                                         qe[:, (2 * j + 1) * P:(2 * j + 2) * P], start=True, stop=True)
                else:
                    for j in range(TT):
                        t = slice(j * P, j * P + P)
                        last = pe.matmul(ps[:, bank, t], ke[:, t], qe[:, t], start=True, stop=True)
                last.then_inc(level_done, 1)
                c.level.n += 1

            def hgrn_levels(h, *ns):
                for n in ns:
                    hgrn_level(h, n)

            def hgrn_out(h):
                pe.wait_ge(level_merged, c.level.at(0))
                pe.wait_ge(op_ready, c.op.at(0))
                d = slice(h * P, h * P + P)
                for j in range(TT):
                    pe.matmul(ps[:, 6, j * P:j * P + P], hg_v[:, j, d], hg_s[:, j, :], start=j == 0, stop=False, skip_group_check=True)
                for j in range(2):
                    pe.matmul(ps[:, 6, (2 * j + 1) * P:(2 * j + 2) * P], hg_v[:, 2 * j, d], hg_p128[:, j, :],
                              start=False, stop=False, skip_group_check=True)
                for j in range(2):
                    last = pe.matmul(ps[:, 6, 256:512], hg_v[:, j, d], hg_p256[:, j, :], start=False, stop=j == 1, skip_group_check=True)
                last.then_inc(head_done, 1)

            values_2(lambda t: None)
            pe.wait_ge(aux_evacuated, c.aux.at(0))
            pe.wait_ge(conv_ready, c.conv.at(1))
            c.conv.n += 1
            for j in range(CT):
                last = pe.matmul(ps[:, 6, :], ones_p, conv_out[:, j, :], start=j == 0, stop=j == CT - 1)
            last.then_inc(mean_done, 1)
            gates()
            stats(CT)
            project(bank_a())
            project(bank_a())
            c.op.n += CT
            pe.wait_ge(op_ready, c.op.at(0))
            project_half(0)
            stats(1, pair_ones[:, :])
            stats(1, pair_ones[:, :])

            for h in range(HG_HEADS):
                if h:
                    gates()
                    stats(1)
                    c.op.n += 1
                    project_half(0)
                if h < HG_HEADS - 1:
                    project(bank_a(), lambda: hgrn_levels(h, 0, 1))
                    hgrn_levels(h, 2, 3, 4)
                    project(bank_a(), lambda: hgrn_levels(h, 5, 6))
                    stats(1, pair_ones[:, :])
                    hgrn_levels(h, 7, 8, 9)
                    stats(1, pair_ones[:, :])
                else:
                    after = ((0, 1), (2, 3, 4), (5, 6), (7, 8, 9))
                    values_2(lambda t: hgrn_levels(h, *after[t]))
                hgrn_out(h)
            stats(1)
            c.op.n += 1

            def sb_pair(g):
                steps = [(i, j) for i in range(2) for j in (3, 2, 1, 0)]

                def z_products(bank, i, j, stop):
                    part = slice(i * SB_DH, i * SB_DH + SB_DH)
                    return pe.matmul(ps[:, bank, 0:SB_W[j]], sb_k[part, g, j * P:j * P + P], sb_q[part, g, j * P:S], start=True, stop=stop)

                def z(i, j):
                    need(pe, sp_ready, c.z.at(-1))
                    z_products(4 + c.z.n % 2, i, j, True).then_inc(z_done, 1)
                    c.z.n += 1

                def arg(i, j):
                    pe.wait_ge(sp_ready, c.arg.at(1))
                    need(pe, a_ready, c.arg.at(-1))
                    bank = 6 + c.arg.n % 2
                    z_products(bank, i, j, False)
                    for e in range(TT - 1, j, -1):
                        pe.matmul(ps[:, bank, (e - j) * P:SB_W[j]], neg_tri[:, 0:1].to_broadcast([P, P]), sb_sp[i][e], start=False, stop=False)
                    pe.matmul(ps[:, bank, 0:SB_W[j]], neg_tri[:, :], sb_sp[i][j], start=False, stop=True).then_inc(arg_done, 1)
                    c.arg.n += 1

                def out(bank, i):
                    part = slice(i * SB_DH, i * SB_DH + SB_DH)
                    pe.wait_ge(a_ready, c.a.at(TT))
                    c.a.n += TT
                    d = (2 * g + i) * SB_DH
                    for j in range(TT):
                        last = pe.matmul(ps[part, bank, j * P:S], sb_v[:, j, d:d + SB_DH], sb_a[i][j], start=j == 0, stop=j == TT - 1)
                    return last

                bank = None

                def step(n):
                    nonlocal bank
                    if n < 8:
                        z(*steps[n])
                    if n >= 2:
                        arg(*steps[n - 2])
                    if n == 7:
                        bank = bank_v()
                        out(bank, 0)

                for m in range(4):
                    project(bank_a(), lambda: step(2 * m))
                    step(2 * m + 1)
                step(8)
                step(9)
                tile(out(bank, 1))

            pe.wait_ge(normalised, c.rt.at(0))
            for g in range(4):
                sb_pair(g)
                if g == 0:
                    pe.wait_ge(op_ready, c.op.at(0))
                project_half(4)
            pe.wait_ge(dve_evacuated, c.dve.at(-2))
            for g in range(4):
                project_half(0)

            project_fresh(bank_v(), bank_v())
            for m in range(2, KT):
                project(bank_v())
            x_stats()

            def mlp_up():
                project(bank_a())
                project(bank_a())

            c.dve.ring = WIDE
            project_fresh(bank_a(), bank_a())
            with loop(pe, MLP_CHUNKS // 3, c, units=12, tiles=30, act=6, dve=24, hid=6):
                for chunk in range(3):
                    mlp_up()
                    down(chunk)
            down(0)

            def ffn():
                def up(first=gates):
                    first()
                    project(bank_v())
                    project(bank_v())

                x_stats()
                c.dve.ring = WIDE
                up(lambda: project_fresh(bank_a(), bank_a()))
                with loop(pe, FFN_CHUNKS // 2, c, units=12, tiles=24, act=4, dve=20, hid=4):
                    up()
                    down(0)
                    up()
                    down(1)
                down(0)
                c.dve.ring = 2

            def lru_gates(pair):
                pe.wait_ge(conv_ready, c.conv.at(1))
                need(pe, aux_evacuated, c.aux.at(0))
                pe.wait_ge(rt_ready, c.rt.at(0))
                if pair == 0:
                    pe.wait_ge(lru_loaded, c.lru.at(16))
                    c.lru.n += 16
                    pe.wait_ge(cum_ready, c.cum.at(1))
                for t in range(2):
                    for n in range(2):
                        last = pe.matmul(ps[:, 4 + 2 * t + n, :], lru_w[:, n, 2 * pair + t, :], xc[:, t, :], start=True, stop=True)
                last.then_inc(gates_done, 1)
                c.conv.n += 1
                c.aux.n += 1

            def attend(g, n):
                if n < 8:
                    i, r = n // 4, n % 4
                    if c.sc.n > 1:
                        pe.wait_ge(exp_ready, c.sc.at(-1))
                    if n == 0:
                        pe.wait_ge(cum_ready, c.cum.at(1))
                        pe.wait_ge(normalised, c.rt.at(0))
                    w = slice(0, (r + 1) * P)
                    pe.matmul(ps[:, 4 + c.sc.n % 2, w], q_h[g % 2][:, i, r * P:r * P + P], k_h[g % 2][:, i, w], start=True, stop=False)
                    h = 2 * g + i
                    pe.matmul(ps[:, 4 + c.sc.n % 2, w], ident[0:HEADS, h:h + 1].to_broadcast([HEADS, P]), neg_cum_f[:, w],
                              start=False, stop=True).then_inc(scores_done, 1)
                    c.sc.n += 1
                if n in (6, 10):
                    i = n // 4 - 1
                    pe.wait_ge(turned_copied, c.pv.at(4))
                    c.pv.n += 4
                    bank = bank_v()
                    for j in range(TT):
                        last = pe.matmul(ps[:, bank, j * P:S], v_h[g % 2][:, j, i * P:i * P + P], probs_t[:, j, j * P:S],
                                         start=j == 0, stop=j == TT - 1)
                    tile(last)
                if 2 <= n <= 9:
                    r = (n - 2) % 4
                    pe.wait_ge(probs_ready, c.turn.at(1))
                    if c.turn.n:
                        pe.wait_ge(turned_copied, c.turn.at(0))
                    for j in range(r + 1):
                        last = pe.transpose(ps[:, 6, j * P:j * P + P], probs[:, c.turn.n % 2, j * P:j * P + P], ident[:, :])
                    last.then_inc(turned, 1)
                    c.turn.n += 1

            def queries_keys_values(g, beside):
                for n in range(4):
                    project(bank_a(), lambda: beside(2 * n))
                    if n:
                        stats(1)
                    beside(2 * n + 1)

                def between(t):
                    if t == 1:
                        stats(1)
                    if t < 3:
                        beside(8 + t)

                values_2(between)

            with loop(pe, LAYERS, c, **PER_LAYER["pe"]):
                ffn()
                x_stats()
                for j in range(4):
                    if j == 0:
                        project_fresh(bank_a(), bank_a())
                        project(4)
                    else:
                        project(bank_a())
                        project(bank_a())
                    if j:
                        lru_gates(j - 1)
                    project(bank_a())
                    project(bank_a())

                def beside_first(n):
                    if n == 2:
                        lru_gates(3)

                queries_keys_values(0, beside_first)
                for m in range(0, KT, 2):
                    gates()
                    if m == 0:
                        c.op.n += KT
                        pe.wait_ge(op_ready, c.op.at(0))
                    project_b()
                    project_b()
                for g in range(1, 4):
                    queries_keys_values(g, lambda n: attend(g - 1, n))
                for m in range(KT):
                    project(bank_a(), lambda: attend(3, 2 * m) if 2 * m < STEPS else None)
                    if 2 * m + 1 < STEPS:
                        attend(3, 2 * m + 1)
                c.op.n += KT
                c.cum.n += 1
                pe.wait_ge(op_ready, c.op.at(0))
                for m in range(KT):
                    project_b()
                project_fresh(bank_v(), bank_v())
                for m in range(2, KT):
                    project(bank_v())
                ffn()

        @block.scalar
        def _(act):
            c = Counts()

            def round_unit(slot, loaded):
                act.wait_ge(raw_loaded[slot], loaded)
                act.activation(w_hi[:, slot, :], raw[:, slot, :], ACT.Copy).then_inc(hi_ready, 1)

            def tick():
                need(act, tiles_done, c.tiles.at(0))
                round_unit((c.units.n + LEAD) % RING, c.units.quarter(LEAD))
                c.units.n += 1

            def evacuate(out, func, bias=0.0, scale=1.0):
                act.wait_ge(tiles_done, c.tiles.at(1))
                act.activation(out, ps[:, c.act.n % 2, :], func, bias=bias, scale=scale).then_inc(act_evacuated, 1)
                c.tiles.n += 1
                c.act.n += 1

            def pass_v(n=1):
                c.tiles.n += n
                c.dve.n += n

            def square(tile):
                need(act, stat_done, c.sq.at(-1))
                act.activation(sq[:, c.sq.n % 2, :], tile, ACT.Square).then_inc(sq_ready, 1)
                c.sq.n += 1

            def inverse_rms(n, late=0):
                act.wait_ge(stat_done, c.sq.at(-late))
                need(act, normalised, c.rt.at(0))
                act.activation(rt, ps[:, 7, :], ACT.Ln, bias=eps_col, scale=1.0 / n)
                act.drain()
                act.activation(rt, rt, ACT.Exp, scale=-0.5).then_inc(rt_ready, 1)
                c.rt.n += 1

            def round_tiles(dst, ks, shift=None):
                need(act, tiles_done, c.tiles.at(0))
                for k in ks:
                    act.wait_ge(t_ready, c.t.at(1))
                    t = tt[:, c.t.n % 2, :]
                    if shift is None:
                        act.activation(dst[:, k, :], t, ACT.Copy).then_inc(op_rounded, 1)
                    else:
                        act.activation(dst[:, k, :], t, ACT.Identity, bias=shift[:, k:k + 1]).then_inc(op_rounded, 1)
                    c.t.n += 1

            def x_square(k):
                if k >= 2:
                    act.wait_ge(x_sq_added, c.sums.at(max(k - 2, 1)))
                act.activation(sq[:, k % 2, :], xres[:, k, :], ACT.Square).then_inc(x_sq_ready, 1)
                if k == KT - 1:
                    c.sums.n += KT - 2
                    c.sq.n += 2

            act.wait_ge(consts_ready, 1)
            act.wait_ge(par_loaded, 16)
            act.wait_ge(c_loaded, 16)
            act.activation(c_act, c_act, ACT.Silu).then_inc(c_ready, 1)
            act.wait_ge(keep_asked, 1)
            act.activation(keep, keep, ACT.Exp).then_inc(keep_ready, 1)
            act.wait_ge(x_loaded, 16)
            for k in range(KT):
                x_square(k)
            inverse_rms(D)
            for u in range(LEAD):
                round_unit(u, 16)
            act.wait_ge(mod_ready, 1)
            round_tiles(a_hi, range(KT), modp[:, 0:KT])

            for j in range(CT):
                tick()
                pass_v()
                tick()
                need(act, dve_evacuated, c.dve.at(-2))
                evacuate(sgate[:, j % 2, :], ACT.Sigmoid)
            for h in range(HG_HEADS):
                tick()
                evacuate(hg_q[:, h, :], ACT.Silu)
            for h in range(HG_HEADS):
                tick()
                evacuate(hg_k[:, h, :], ACT.Sigmoid, scale=-1.0)

            def values_4(dst):
                for u in range(4):
                    tick()
                    c.tiles.n += 1
                act.wait_ge(tiles_done, c.tiles.at(0))
                for t in range(TT):
                    last = act.activation(dst[:, t, :], ps[:, 4 + t, :], ACT.Copy)
                last.then_inc(aux_evacuated, 1)

            values_4(hg_v)
            for h in range(HG_HEADS):
                tick()
                evacuate(hg_g[:, h, :], ACT.Silu)

            def gates(table, name, first):
                for m in range(2):
                    tick()
                    need(act, dve_evacuated, c.dve.at(0))
                    evacuate(sgate[:, m, :], ACT.Sigmoid, bias=par(table, name, first + m))

            def hgrn_log():
                act.wait_ge(log_asked, c.log.at(1))
                c.log.n += 1
                act.activation(hg_log, hg_log, ACT.Ln).then_inc(log_ready, 1)

            def hgrn_decays(*ns):
                for n in ns:
                    act.wait_ge(decay_asked, c.decay.at(1))
                    c.decay.n += 1
                    act.activation(hg_e[:, n % 2, :], hg_e[:, n % 2, :], ACT.Exp).then_inc(decay_ready, 1)

            def sb_value(group, b):
                out = sb_v[:, 2 * b:2 * b + 2, group * 2 * P:(group + 1) * 2 * P]
                act.wait_ge(tiles_done, c.tiles.at(1))
                act.activation(out, ps[:, c.act.n % 2, :].rearrange("p (t d) -> p t d", t=2), ACT.Copy).then_inc(act_evacuated, 1)
                c.tiles.n += 1
                c.act.n += 1

            def sb_operand(dst):
                evacuate(dst, ACT.Copy)
                act.drain()
                square(dst)

            tick()
            sb_value(0, 0)
            sb_value(0, 1)
            tick()
            gates(PAR1, "gate_b", 0)
            for j in range(CT):
                act.wait_ge(centred, j + 1)
                square(conv_out[:, j, :])
            inverse_rms(CONV_CH)
            tick()
            for j in range(CT):
                act.wait_ge(t_ready, c.t.at(1))
                t = tt[:, c.t.n % 2, :]
                act.activation(t, t, ACT.Silu, scale=par(PAR1, "ln_g", j), bias=par(PAR1, "ln_b", j))
                act.drain()
                act.activation(b_hi[:, j, :], t, ACT.Copy).then_inc(op_rounded, 1)
                c.t.n += 1
            sb_operand(sb_q[:, 0, :])
            tick()
            sb_operand(sb_k[:, 0, :])
            tick()
            pass_v(2)
            inverse_rms(SB_DH, 1)
            inverse_rms(SB_DH)

            for h in range(HG_HEADS):
                if h:
                    gates(PAR1, "gate_b", 2 * h)
                    inverse_rms(P)
                    round_tiles(b_hi, [4 + h - 1])
                    tick()
                    pass_v(2)
                hgrn_log()
                tick()
                hgrn_decays(0, 1, 2, 3)
                if h < HG_HEADS - 1:
                    sb_operand(sb_q[:, h + 1, :])
                    hgrn_decays(4, 5)
                    tick()
                    hgrn_decays(6, 7)
                    sb_operand(sb_k[:, h + 1, :])
                    inverse_rms(SB_DH, 1)
                    hgrn_decays(8)
                    inverse_rms(SB_DH)
                else:
                    sb_value(1, 0)
                    hgrn_decays(4, 5, 6, 7)
                    sb_value(1, 1)
                    tick()
                    hgrn_decays(8)
                act.wait_ge(head_done, h + 1)
                square(ps[:, 6, :])
            inverse_rms(P)
            round_tiles(b_hi, [7])

            def sb_step(n):
                steps = [(i, j) for i in range(2) for j in (3, 2, 1, 0)]
                if n < 8:
                    i, j = steps[n]
                    e = sb_e[c.z.n % 2][:, 0:SB_W[j]]
                    act.wait_ge(neg_abs_ready, c.z.at(1))
                    act.activation(e, e, ACT.Exp)
                    act.drain()
                    act.activation(e, e, ACT.Ln, bias=one_col).then_inc(log1p_ready, 1)
                    c.z.n += 1
                if n >= 2:
                    i, j = steps[n - 2]
                    b = c.a.n % 2
                    act.wait_ge(diag_ready, c.a.at(1))
                    if j < TT - 1:
                        act.activation(sb_a[i][j][:, P:SB_W[j]], ps[:, 6 + b, P:SB_W[j]], ACT.Exp)
                    act.activation(sb_a[i][j][:, 0:P], sb_diag[b], ACT.Exp).then_inc(a_ready, 1)
                    c.a.n += 1

            for g in range(4):
                for m in range(4):
                    tick()
                    sb_step(2 * m)
                    if m == 0:
                        act.wait_ge(dve_evacuated, c.dve.at(0))
                    gate, first = (sgate[:, m, :], KT) if m < 2 else (sb_gate(2 * g + m - 2), 2 * KT)
                    evacuate(gate, ACT.Identity, bias=par(PAR1, "gate_b", first + 2 * g + m % 2))
                    sb_step(2 * m + 1)
                sb_step(8)
                sb_step(9)
                act.drain()
                act.activation(sgate[:, :, :], sgate[:, :, :], ACT.Sigmoid).then_inc(sigmoid_ready, 1)
                act.wait_ge(tiles_done, c.tiles.at(1))
                act.activation(b_hi[:, g, :], ps[:, 2 + c.dve.n % 2, :], ACT.Copy).then_inc(op_rounded, 1)
                pass_v()
                tick()
                pass_v(2)
            for half in (hg_q, hg_v):
                act.activation(half, half, ACT.Sigmoid).then_inc(sigmoid_ready, 1)
            for g in range(4):
                tick()
                pass_v(2)

            def round_merged(merged):
                need(act, tiles_done, c.tiles.at(0))
                for k in range(KT):
                    act.wait_ge(merged_ready, c.merged.at(1))
                    act.activation(a_hi[:, k, :], merged[:, k, :], ACT.Copy).then_inc(op_rounded, 1)
                    c.merged.n += 1

            def project_v(n):
                for m in range(n):
                    tick()
                    pass_v()

            def final_project():
                act.activation(cols[:, 125:126], one_col, ACT.Ln)
                for m in range(KT):
                    tick()
                    pass_v()
                    if m >= 2:
                        act.wait_ge(dve_evacuated, c.dve.at(-2))
                        x_square(m - 2)

            def final_down():
                act.activation(cols[:, 125:126], one_col, ACT.Ln)
                tick()
                pass_v(4)
                for k in range(2):
                    act.wait_ge(dve_evacuated, c.dve.at(k - 3))
                    x_square(k)
                tick()
                pass_v(4)

            def norm(shift=None, squared=KT - 2):
                for k in range(squared, KT):
                    act.wait_ge(dve_evacuated, c.dve.at(k + 1 - KT))
                    x_square(k)
                inverse_rms(D)
                round_tiles(a_hi, range(KT), shift)

            round_merged(xres)
            c.op.n += KT + 4 + HG_HEADS + KT
            act.wait_ge(op_ready, c.op.at(0))
            act.dma_start(xres[:, :, :], x_t).then_inc(x_loaded, 16)
            final_project()
            norm(modp[:, 3 * KT:4 * KT])

            def down():
                for u in range(2):
                    tick()
                    pass_v(4)

            def mlp_up():
                for m in range(2):
                    tick()
                    need(act, hidden_ready, c.hid.at(0))
                    evacuate(sgate[:, m, :], ACT.Relu)
                c.hid.n += 2

            mlp_up()
            with loop(act, MLP_CHUNKS // 3, c, units=12, tiles=30, act=6, dve=24, hid=6):
                for chunk in range(3):
                    mlp_up()
                    down()
            down()
            c.op.n += KT
            c.conv.n += 1

            def ffn(down_last):
                def up():
                    for m in range(2):
                        tick()
                        need(act, dve_evacuated, c.dve.at(0))
                        evacuate(sgate[:, m, :], ACT.Silu)
                    project_v(2)

                up()
                with loop(act, FFN_CHUNKS // 2, c, units=12, tiles=24, act=4, dve=20):
                    up()
                    down()
                    up()
                    down()
                down_last()

            def recurrent_gates(pair):
                act.wait_ge(gates_done, c.gates.at(1))
                c.gates.n += 1
                if pair == 0:
                    act.wait_ge(spl_ready, c.spl.at(1))
                    c.spl.n += 1
                act.wait_ge(op_ready, c.op.at(0))
                for t in range(2):
                    act.activation(rr[:, t, :], ps[:, 4 + 2 * t, :], ACT.Tanh, scale=0.5, bias=half_ba[:, 2 * pair + t:2 * pair + t + 1])
                    last = act.activation(ii[:, t, :], ps[:, 5 + 2 * t, :], ACT.Tanh, scale=0.5,
                                          bias=half_bx[:, 2 * pair + t:2 * pair + t + 1])
                last.then_inc(aux_evacuated, 1)
                act.drain()
                for t in range(2):
                    neg = tmp8[:, 2 * pair + t:2 * pair + t + 1]
                    act.activation(th[:, t, :], rr[:, t, :], ACT.Tanh, scale=neg, bias=neg)
                act.drain()
                for t in range(2):
                    pos = half_spl[:, 2 * pair + t:2 * pair + t + 1]
                    last = act.activation(rr[:, t, :], rr[:, t, :], ACT.Exp, scale=pos, bias=pos)
                last.then_inc(lru_ready, 1)

            def recurrent_root():
                act.wait_ge(root_asked, c.root.at(1))
                c.root.n += 1
                act.activation(th, th, ACT.Sqrt, scale=0.25).then_inc(root_ready, 1)

            def recurrent_out(pair):
                round_tiles(b_hi, [2 * pair, 2 * pair + 1])
                c.op.n += 2

            def attend(g, n):
                if n < 8:
                    b, w = c.exp.n % 2, slice(0, (n % 4 + 1) * P)
                    act.wait_ge(max_ready, c.exp.at(1))
                    if c.exp.n > 1:
                        act.wait_ge(turned, c.exp.at(-1))
                    act.activation(probs[:, b, w], ps[:, 4 + b, w], ACT.Exp, bias=neg_max[:, b:b + 1],
                                   accum_out=den[:, b:b + 1]).then_inc(exp_ready, 1)
                    c.exp.n += 1
                if n in (6, 10):
                    pass_v()
                if 2 <= n <= 9:
                    r = (n - 2) % 4
                    act.wait_ge(turned, c.turn.at(1))
                    c.turn.n += 1
                    if r == 0:
                        act.wait_ge(tiles_done, c.tiles.at(0))
                    act.activation(probs_t[:, 0:r + 1, r * P:r * P + P],
                                   ps[:, 6, 0:(r + 1) * P].rearrange("p (j t) -> p j t", t=P), ACT.Copy).then_inc(turned_copied, 1)
                if n in (7, 10):
                    round_tiles(b_hi, [2 * g + (n == 10)])

            def queries_keys_values(g, beside):
                for n in range(4):
                    tick()
                    beside(2 * n)
                    dst, name = ((q_h, "b_q"), (k_h, "b_k"))[n // 2]
                    dst = dst[g % 2][:, n % 2, :]
                    evacuate(dst, ACT.Identity, bias=par(PAR2, name, 2 * g + n % 2))
                    act.drain()
                    square(dst)
                    if n:
                        inverse_rms(P, 1)
                    beside(2 * n + 1)
                tick()
                for t in range(TT):
                    if t == 3:
                        beside(10)
                    if t % 2:
                        evacuate(v_h[g % 2][:, t - 1:t + 1, :].rearrange("p t d -> p (t d)"), ACT.Copy)
                    if t == 1:
                        inverse_rms(P)
                        beside(9)
                    if t == 0:
                        beside(8)
                tick()

            with loop(act, LAYERS, c, **PER_LAYER["act"]) as layer:
                act.wait_ge(dve_evacuated, c.dve.at(-KT))
                act.dma_start(params[:, 0:N_PAR2], par2[bass.ds(layer, 1)].rearrange("o p n -> p (o n)")).then_inc(par_loaded, 16)
                act.dma_start(arena[:, 0:2 * KT * P], lru[bass.ds(layer, 1)].rearrange("o p n -> p (o n)")).then_inc(lru_loaded, 16)
                norm(squared=0)
                act.wait_ge(par_loaded, c.par.at(32))
                c.par.n += 16
                act.activation(tmp8, par(PAR2, "lam", 0, KT), ACT.Abs)
                act.drain()
                act.activation(tmp8, tmp8, ACT.Exp, scale=-1.0)
                act.drain()
                act.activation(tmp8, tmp8, ACT.Ln, bias=one_col).then_inc(spl_logged, 1)
                ffn(final_down)
                norm(squared=2)
                for j in range(4):
                    for t in range(2):
                        tick()
                        if t == 0:
                            need(act, conv_ready, c.conv.at(0))
                        evacuate(xr[:, t, TAPS_2 - 1:TAPS_2 - 1 + S], ACT.Identity, bias=par(PAR2, "b_xr", 2 * j + t))
                    if j == 0:
                        tick()
                        c.tiles.n += 1
                        act.wait_ge(f_asked, c.f.at(1))
                        c.f.n += 1
                        act.activation(f_abs, f_row, ACT.Abs)
                        act.drain()
                        act.activation(f_abs, f_abs, ACT.Exp, scale=-1.0)
                        act.drain()
                        act.activation(f_abs, f_abs, ACT.Ln, bias=one_col[0:HEADS, :]).then_inc(f_logged, 1)
                        c.op.n += 2 * KT
                    c.conv.n += 1
                    if j:
                        recurrent_gates(j - 1)
                    tick()
                    evacuate(gr[:, j % 2, 0, :], ACT.Gelu_apprx_tanh, bias=par(PAR2, "b_gr", 2 * j))
                    if j:
                        recurrent_root()
                    tick()
                    evacuate(gr[:, j % 2, 1, :], ACT.Gelu_apprx_tanh, bias=par(PAR2, "b_gr", 2 * j + 1))
                    if j:
                        recurrent_out(j - 1)

                def beside_first(n):
                    if n == 2:
                        recurrent_gates(3)
                    if n == 4:
                        recurrent_root()
                    if n == 5:
                        recurrent_out(3)

                queries_keys_values(0, beside_first)
                for m in range(0, KT, 2):
                    gates(PAR2, "b_gn", m)
                    project_v(2)
                for g in range(1, 4):
                    queries_keys_values(g, lambda n: attend(g - 1, n))
                for m in range(KT):
                    tick()
                    if 2 * m < STEPS:
                        attend(3, 2 * m)
                    need(act, dve_evacuated, c.dve.at(-1))
                    evacuate(attn_gate(m), ACT.Sigmoid, bias=par(PAR2, "b_ga", m))
                    if 2 * m + 1 < STEPS:
                        attend(3, 2 * m + 1)
                project_v(KT)
                round_merged(merged2)
                c.op.n += 2 * KT
                final_project()
                norm()
                ffn(down)
                c.op.n += KT

        @block.vector
        def _(dve):
            c = Counts()

            def v_tile():
                dve.wait_ge(tiles_done, c.tiles.at(1))
                c.tiles.n += 1
                c.dve.n += 1
                return ps[:, 2 + (c.dve.n - 1) % c.dve.ring, :]

            def pass_a(n=1):
                c.tiles.n += n
                c.act.n += n

            def low_part(dst, src_hi, tile):
                dve.wait_ge(op_rounded, c.rounded.at(1))
                c.rounded.n += 1
                return dve.tensor_tensor(dst, tile, src_hi.bitcast(F32), ALU.subtract)

            def add_square(k):
                if k == 0 or k == KT - 1:
                    return
                dve.wait_ge(x_sq_ready, c.squares.at(k + 1))
                dve.tensor_tensor(sq_sum, sq[:, 0, :] if k == 1 else sq_sum, sq[:, k % 2, :], ALU.add).then_inc(x_sq_added, 1)
                dve.drain()

            def norm(scale, shift=None):
                c.squares.n += KT
                dve.wait_ge(rt_ready, c.rt.at(1))
                c.rt.n += 1

                def scaled(k):
                    ins = dve.scalar_tensor_tensor(tt[:, (c.t.n + k) % 2, :], xres[:, k, :], scale[:, k:k + 1], rt, ALU.mult, ALU.mult)
                    return ins.then_inc(t_ready, 1)

                scaled(0)
                dve.drain()
                for k in range(KT):
                    if k + 1 < KT:
                        scaled(k + 1)
                    else:
                        dve.memset(cols[:, 126:127], 0.0).then_inc(normalised, 1)
                    t = tt[:, (c.t.n + k) % 2, :]
                    if shift is None:
                        low_part(a_lo[:, k, :], a_hi[:, k, :], t).then_inc(op_ready, 1)
                    else:
                        dve.wait_ge(op_rounded, c.rounded.at(1))
                        c.rounded.n += 1
                        dve.scalar_tensor_tensor(a_lo[:, k, :], t, shift[:, k:k + 1], a_hi[:, k, :].bitcast(F32), ALU.add, ALU.subtract
                                                 ).then_inc(op_ready, 1)
                    dve.drain()
                c.t.n += KT

            dve.wait_ge(consts_ready, 1)
            dve.wait_ge(par_loaded, 16)
            lb = par(PAR1, "lb", 0, HG_HEADS)
            dve.tensor_tensor(keep, lb, lb, ALU.subtract).then_inc(keep_asked, 1)
            dve.wait_ge(keep_ready, 1)
            dve.reciprocal(tmp8[:, 0:4], keep)
            dve.drain()
            dve.tensor_tensor(keep, keep, tmp8[:, 0:4], ALU.mult)
            dve.drain()
            dve.tensor_tensor(keep, keep, keep, ALU.subtract)
            dve.drain()
            dve.tensor_scalar(keep, keep, -1.0, 1.0, ALU.mult, ALU.add)
            for k in range(KT):
                add_square(k)
            dve.wait_ge(c_ready, 1)
            with dve.Fori(0, MODS // MOD_RING) as i:
                for s in range(MOD_RING):
                    dve.wait_ge(mod_loaded[s], i * 16 + 16)
                    dve.scalar_tensor_tensor(mod_stage[:, s, :], mod_stage[:, s, :], 1.0, c_act, ALU.mult, ALU.mult,
                                             accum_out=modp[:, bass.ds(i * MOD_RING + s, 1)]).then_inc(mod_used, 1)
            dve.drain()
            dve.tensor_tensor(modp, modp, par(PAR1, "mod_b", 0, MODS), ALU.add).then_inc(mod_ready, 1)
            dve.drain()
            for dst, at, g in ((scale1, 1, "norm1_g"), (scale2, 4, "norm2_g")):
                dve.scalar_tensor_tensor(dst, modp[:, at * KT:(at + 1) * KT], 1.0, par(PAR1, g, 0, KT), ALU.add, ALU.mult)
            dve.tensor_scalar(q_col, par(PAR1, "sbq_g"), SB_DH ** -0.5, None, ALU.mult)
            dve.memset(conv_in[:, :, 0:PAD], 0.0)
            dve.memset(hg_s, 0.0)
            dve.drain()
            norm(scale1, modp[:, 0:KT])

            for j in range(CT):
                a = v_tile()
                pass_a()
                dve.wait_ge(act_evacuated, c.act.at(0))
                dve.tensor_tensor(conv_in[:, j, PAD:PAD + S], a, sgate[:, j % 2, :], ALU.mult).then_inc(dve_evacuated, 1)
            dve.drain()
            taps = PAR1["conv_w"][0]
            for j in range(CT):
                dve.tensor_scalar(conv_out[:, j, :], conv_in[:, j, 0:S], params[:, taps + j:taps + j + 1], par(PAR1, "conv_b", j),
                                  ALU.mult, ALU.add)
            with dve.Fori(1, TAPS) as tap:
                dve.drain()
                for j in range(CT):
                    dve.scalar_tensor_tensor(conv_out[:, j, :], conv_in[:, j, bass.ds(tap, S)], params[:, bass.ds(tap * CT + (taps + j), 1)],
                                             conv_out[:, j, :], ALU.mult, ALU.add)
            dve.drain()
            dve.memset(cols[:, 126:127], 0.0).then_inc(conv_ready, 1)

            pass_a(2 * HG_HEADS)
            c.tiles.n += 4
            pass_a(HG_HEADS + 2 + 2 + 2)
            dve.wait_ge(mean_done, 1)
            for j in range(CT):
                dve.scalar_tensor_tensor(conv_out[:, j, :], ps[:, 6, :], -1.0 / CONV_CH, conv_out[:, j, :], ALU.mult, ALU.add
                                         ).then_inc(centred, 1)
            dve.drain()
            dve.wait_ge(rt_ready, c.rt.at(1))
            c.rt.n += 1

            def ln_scaled(j):
                ins = dve.tensor_tensor(tt[:, (c.t.n + j) % 2, :], conv_out[:, j, :], rt, ALU.mult).then_inc(t_ready, 1)

            def ln_low(j):
                low_part(b_lo[:, j, :], b_hi[:, j, :], tt[:, (c.t.n + j) % 2, :]).then_inc(op_ready, 1)
                dve.drain()

            ln_scaled(0)
            ln_scaled(1)
            ln_low(0)
            ln_scaled(2)
            ln_low(1)
            ln_scaled(3)
            ln_low(2)
            ln_low(3)
            c.t.n += CT
            dve.memset(cols[:, 126:127], 0.0).then_inc(normalised, 1)

            def sb_normalise(t, col):
                dve.wait_ge(rt_ready, c.rt.at(1))
                c.rt.n += 1
                dve.scalar_tensor_tensor(t, t, col, rt, ALU.mult, ALU.mult).then_inc(normalised, 1)

            sb_normalise(sb_q[:, 0, :], q_col)
            sb_normalise(sb_k[:, 0, :], par(PAR1, "sbk_g"))

            def hgrn_head(h):
                q, k = hg_q[:, h, :], hg_k[:, h, :]
                dve.drain()
                dve.tensor_scalar(k, k, keep[:, h:h + 1], None, ALU.mult)
                dve.drain()
                dve.tensor_scalar(hg_log, k, -1.0, 1.0, ALU.mult, ALU.add).then_inc(log_asked, 1)
                dve.wait_ge(log_ready, h + 1)
                dve.tensor_tensor_scan(hg_b64, reset64, hg_log, 0.0, ALU.mult, ALU.add)
                for e in range(2):
                    part = slice(e * 256, e * 256 + 256)
                    dve.tensor_tensor_scan(hg_b256[:, part], ones[:, part], hg_log[:, part], 0.0, ALU.mult, ALU.add)
                dve.drain()

                def exponents(n):
                    m = LEVELS[n]
                    b = (hg_b256 if m >= 128 else hg_b64).rearrange("p (b h i) -> p b h i", h=2, i=m)
                    e = hg_e[:, n % 2, :].rearrange("p (b h i) -> p b h i", h=2, i=m)
                    middle = b[:, :, 0, m - 1:m].to_broadcast([P, S // (2 * m), m])
                    if m in (256, 64):
                        dve.tensor_copy(e[:, :, 1, :], b[:, :, 1, :])
                    else:
                        dve.tensor_tensor(e[:, :, 1, :], b[:, :, 1, :], middle, ALU.subtract)
                    dve.tensor_tensor(e[:, :, 0, :], middle, b[:, :, 0, :], ALU.subtract).then_inc(decay_asked, 1)

                def decayed(n):
                    dve.wait_ge(decay_ready, c.decay.at(1))
                    c.decay.n += 1
                    if n >= 2:
                        dve.wait_ge(level_done, c.level.at(n - 1))
                    dve.tensor_tensor(hg_qe[:, n % 2, :], q, hg_e[:, n % 2, :], ALU.mult)
                    dve.tensor_tensor(hg_ke[:, n % 2, :], k, hg_e[:, n % 2, :], ALU.mult).then_inc(level_ready, 1)
                    dve.drain()

                def merge(n):
                    dve.wait_ge(level_done, c.level.at(n + 1))
                    got = ps[:, 4 + (c.level.n + n) % 2, :]
                    if n == 0 and h:
                        dve.wait_ge(head_done, h)
                    if n < 2:
                        into = (hg_p256, hg_p128)[n].rearrange("p j t -> p (j t)")
                        ins = dve.tensor_copy(into, got[:, 0:(S, 2 * P)[n]])
                    else:
                        mask = masks[:, n - 2:n - 1, :].to_broadcast([P, TT, P])
                        ins = dve.copy_predicated(hg_s, mask, got.rearrange("p (j t) -> p j t", t=P))
                        dve.drain()
                    ins.then_inc(level_merged, 1)

                exponents(0)
                exponents(1)
                for n in range(len(LEVELS)):
                    decayed(n)
                    if n + 2 < len(LEVELS):
                        exponents(n + 2)
                    if n:
                        merge(n - 1)
                if h < HG_HEADS - 1:
                    sb_normalise(sb_q[:, h + 1, :], q_col)
                merge(len(LEVELS) - 1)
                merge(len(LEVELS))
                c.level.n += len(LEVELS) + 1
                if h < HG_HEADS - 1:
                    sb_normalise(sb_k[:, h + 1, :], par(PAR1, "sbk_g"))

            def hgrn_norm(h):
                dve.wait_ge(rt_ready, c.rt.at(1))
                c.rt.n += 1
                t = tt[:, c.t.n % 2, :]
                dve.tensor_tensor(t, ps[:, 6, :], rt, ALU.mult).then_inc(normalised, 1)
                dve.drain()
                dve.scalar_tensor_tensor(t, t, par(PAR1, "hg_g"), hg_g[:, h, :], ALU.mult, ALU.mult).then_inc(t_ready, 1)
                dve.drain()
                low_part(b_lo[:, 4 + h, :], b_hi[:, 4 + h, :], t).then_inc(op_ready, 1)
                dve.drain()
                c.t.n += 1

            def gated(merged, m, first, gate=None):
                y = v_tile()
                g = sgate[:, m % 2, :] if gate is None else gate
                if first:
                    dve.tensor_tensor(merged[:, m, :], g, y, ALU.mult).then_inc(dve_evacuated, 1)
                    return
                dve.tensor_tensor(g, g, y, ALU.mult)
                dve.drain()
                dve.tensor_tensor(merged[:, m, :], merged[:, m, :], g, ALU.add).then_inc(dve_evacuated, 1)

            for h in range(HG_HEADS):
                if h:
                    pass_a(2)
                    hgrn_norm(h - 1)
                hgrn_head(h)
                dve.wait_ge(act_evacuated, c.act.at(0))
                gated(xres, 2 * h, True)
                gated(xres, 2 * h + 1, True)
                pass_a(2)
            hgrn_norm(HG_HEADS - 1)

            def sb_pair():
                steps = [(i, j) for i in range(2) for j in (3, 2, 1, 0)]
                need(dve, arg_done, c.arg.at(0))
                for n in range(10):
                    if n < 8:
                        i, j = steps[n]
                        z, e = ps[:, 4 + c.z.n % 2, 0:SB_W[j]], sb_e[c.z.n % 2][:, 0:SB_W[j]]
                        dve.drain()
                        dve.wait_ge(z_done, c.z.at(1))
                        t = sb_sp[i][j]
                        dve.tensor_scalar(t, z, 0.0, None, ALU.max)
                        dve.drain()
                        dve.scalar_tensor_tensor(e, t, -2.0, z, ALU.mult, ALU.add).then_inc(neg_abs_ready, 1)
                    if n >= 2:
                        b = c.arg.n % 2
                        dve.wait_ge(arg_done, c.arg.at(1))
                        need(dve, a_ready, c.arg.at(-1))
                        dve.scalar_tensor_tensor(sb_diag[b], ps[:, 6 + b, 0:P], 0.0, hide_ge[:, :], ALU.min, ALU.add).then_inc(diag_ready, 1)
                        c.arg.n += 1
                    if n < 8:
                        dve.wait_ge(log1p_ready, c.z.at(1))
                        dve.tensor_tensor(t, t, e, ALU.add)
                        dve.drain()
                        dve.tensor_tensor(t[:, 0:P], t[:, 0:P], before[:, :], ALU.mult).then_inc(sp_ready, 1)
                        c.z.n += 1

            dve.drain()
            for g in range(4):
                pass_a(4)
                sb_pair()
                o = v_tile()
                low_part(b_lo[:, g, :], b_hi[:, g, :], o).then_inc(dve_evacuated, 1)
                dve.wait_ge(sigmoid_ready, g + 1)
                gated(xres, 2 * g, False)
                gated(xres, 2 * g + 1, False)
            dve.wait_ge(sigmoid_ready, 6)
            for m in range(KT):
                gated(xres, m, False, sb_gate(m))

            def split_merged(merged):
                dve.drain()
                dve.memset(cols[:, 126:127], 0.0).then_inc(merged_ready, KT)
                for k in range(KT):
                    low_part(a_lo[:, k, :], a_hi[:, k, :], merged[:, k, :]).then_inc(op_ready, 1)

            split_merged(xres)
            dve.wait_ge(x_loaded, 32)

            def add_tiles(scales, squares=False):
                for m, scale in scales:
                    y = v_tile()
                    dve.scalar_tensor_tensor(xres[:, m, :], y, scale, xres[:, m, :], ALU.mult, ALU.add).then_inc(dve_evacuated, 1)
                    if squares and m:
                        add_square(m - 1)

            add_tiles([(m, modp[:, 2 * KT + m:2 * KT + m + 1]) for m in range(KT)], True)
            dve.drain()
            norm(scale2, modp[:, 3 * KT:4 * KT])

            def hidden(part, m, t):
                n = 2 * part + m
                dve.drain()
                dve.tensor_copy(b_hi[:, n, :], t)
                dve.drain()
                dve.tensor_tensor(b_lo[:, n, :], t, b_hi[:, n, :].bitcast(F32), ALU.subtract).then_inc(hidden_ready, 1)

            def mlp_up(half):
                for m in range(2):
                    pass_a()
                    dve.wait_ge(act_evacuated, c.act.at(0))
                    t = tt[:, m, :]
                    dve.tensor_tensor(t, sgate[:, m, :], sgate[:, m, :], ALU.mult)
                    hidden(half, m, t)

            def mlp_down():
                dve.drain()
                add_tiles([(m, modp[:, 5 * KT + m:5 * KT + m + 1]) for m in range(KT)])

            c.dve.ring = WIDE
            mlp_up(0)
            with loop(dve, MLP_CHUNKS // 3, c, tiles=30, act=6, dve=24):
                for chunk in range(3):
                    mlp_up((chunk + 1) % 3)
                    mlp_down()
            mlp_down()

            def ffn(squares):
                c.dve.ring = WIDE

                def up(half):
                    pass_a(2)
                    for m in range(2):
                        dve.drain()
                        y = v_tile()
                        dve.wait_ge(act_evacuated, c.act.at(0))
                        t = tt[:, m, :]
                        dve.tensor_tensor(t, sgate[:, m, :], y, ALU.mult).then_inc(dve_evacuated, 1)
                        hidden(half, m, t)

                def down(squares=False):
                    dve.drain()
                    add_tiles([(m, 0.5) for m in range(KT)], squares)

                up(0)
                with loop(dve, FFN_CHUNKS // 2, c, tiles=24, act=4, dve=20):
                    up(1)
                    down()
                    up(0)
                    down()
                down(squares)
                c.dve.ring = 2

            def conv4(pair):
                dve.drain()
                dve.wait_ge(act_evacuated, c.act.at(0))
                for n in range(TAPS_2):
                    for t in range(2):
                        j = 2 * pair + t
                        w = par(PAR2, "conv_w", n * KT + j)
                        if n == 0:
                            ins = dve.tensor_scalar(xc[:, t, :], xr[:, t, 0:S], w, par(PAR2, "conv_b", j), ALU.mult, ALU.add)
                        else:
                            ins = dve.scalar_tensor_tensor(xc[:, t, :], xr[:, t, n:n + S], w, xc[:, t, :], ALU.mult, ALU.add)
                    if n < TAPS_2 - 1:
                        dve.drain()
                ins.then_inc(conv_ready, 1)

            def recurrence(pair):
                dve.wait_ge(lru_ready, c.lru.at(1))
                dve.scalar_tensor_tensor(ii, ii, 1.0, xc, ALU.add, ALU.mult)
                dve.drain()
                dve.tensor_tensor(xc, rr, rr, ALU.mult)
                dve.drain()
                dve.scalar_tensor_tensor(th, xc, 1.0, th, ALU.add, ALU.mult).then_inc(root_asked, 1)
                dve.wait_ge(root_ready, c.lru.at(1))
                dve.tensor_tensor(ii, ii, th, ALU.mult)
                dve.drain()
                for t in range(2):
                    dve.tensor_tensor_scan(th[:, t, :], rr[:, t, :], ii[:, t, :], 0.0, ALU.mult, ALU.add)
                dve.drain()
                dve.wait_ge(act_evacuated, c.act.at(0))
                for t in range(2):
                    dve.tensor_tensor(tt[:, t, :], th[:, t, :], gr[:, pair % 2, t, :], ALU.mult).then_inc(t_ready, 1)
                dve.drain()
                for t in range(2):
                    k = 2 * pair + t
                    low_part(b_lo[:, k, :], b_hi[:, k, :], tt[:, t, :]).then_inc(op_ready, 1)
                dve.drain()
                c.t.n += 2
                c.lru.n += 1

            def normalise(dst, col):
                dve.wait_ge(rt_ready, c.rt.at(1))
                c.rt.n += 1
                dve.scalar_tensor_tensor(dst, dst, col, rt, ALU.mult, ALU.mult).then_inc(normalised, 1)

            def attend(g, n):
                if n < 8:
                    r, b = n % 4, c.sc.n % 2
                    bank = ps[:, 4 + b, :]
                    dve.wait_ge(scores_done, c.sc.at(1))
                    c.sc.n += 1
                    dve.tensor_tensor(bank[:, r * P:r * P + P], bank[:, r * P:r * P + P], hide_gt[:, :], ALU.add)
                    dve.drain()
                    dve.tensor_reduce(neg_max[:, b:b + 1], bank[:, 0:(r + 1) * P], AX_X, ALU.max, negate=True).then_inc(max_ready, 1)
                if 1 <= n <= 8:
                    r, b = (n - 1) % 4, c.pr.n % 2
                    dve.wait_ge(exp_ready, c.pr.at(1))
                    c.pr.n += 1
                    dve.reciprocal(den[:, b:b + 1], den[:, b:b + 1])
                    dve.drain()
                    p = probs[:, b, 0:(r + 1) * P]
                    dve.tensor_scalar(p, p, den[:, b:b + 1], None, ALU.mult).then_inc(probs_ready, 1)
                if n in (6, 10):
                    dve.drain()
                    o = v_tile()
                    dve.tensor_scalar(tt[:, c.t.n % 2, :], o, par(PAR2, "b_v", 2 * g + n // 4 - 1), None, ALU.add).then_inc(dve_evacuated, 1)
                    dve.drain()
                    dve.memset(cols[:, 126:127], 0.0).then_inc(t_ready, 1)
                    c.t.n += 1
                if n in (7, 10):
                    h = 2 * g + (n == 10)
                    low_part(b_lo[:, h, :], b_hi[:, h, :], tt[:, (c.t.n - 1) % 2, :]).then_inc(op_ready, 1)
                    dve.drain()

            def queries_keys_values(g, beside):
                for n in range(4):
                    beside(2 * n)
                    pass_a()
                    if n:
                        done = n - 1
                        normalise((q_h, k_h)[done // 2][g % 2][:, done % 2, :], q_col if done < 2 else par(PAR2, "k_g"))
                    beside(2 * n + 1)
                beside(8)
                pass_a()
                normalise(k_h[g % 2][:, 1, :], par(PAR2, "k_g"))
                beside(9)
                beside(10)
                pass_a()

            with loop(dve, LAYERS, c, **PER_LAYER["dve"]):
                dve.wait_ge(par_loaded, c.par.at(32))
                c.par.n += 16
                for k in range(KT):
                    add_square(k)
                norm(par(PAR2, "ffn1_g", 0, KT))
                dve.wait_ge(spl_logged, c.spl.at(1))
                lam = par(PAR2, "lam", 0, KT)
                dve.tensor_scalar(spl, lam, -1.0, 0.0, ALU.mult, ALU.max)
                dve.tensor_scalar(half_ba, par(PAR2, "b_a", 0, KT), 0.5, None, ALU.mult)
                dve.tensor_scalar(half_bx, par(PAR2, "b_x", 0, KT), 0.5, None, ALU.mult)
                dve.tensor_scalar(q_col, par(PAR2, "q_g"), P ** -0.5, None, ALU.mult)
                dve.drain()
                dve.tensor_tensor(spl, spl, tmp8, ALU.add)
                dve.drain()
                dve.tensor_scalar(half_spl, spl, -0.5 * LRU_C, None, ALU.mult)
                dve.tensor_scalar(tmp8, spl, 0.5 * LRU_C, None, ALU.mult).then_inc(spl_ready, 1)
                c.spl.n += 1
                dve.drain()
                ffn(True)
                dve.drain()
                dve.memset(xr[:, :, 0:TAPS_2 - 1], 0.0)
                norm(par(PAR2, "mix_g", 0, KT))
                for j in range(4):
                    pass_a(2)
                    if j == 0:
                        c.tiles.n += 1
                        dve.wait_ge(tiles_done, c.tiles.at(0))
                        dve.tensor_scalar(f_row, ps[0:HEADS, 4, :], par(PAR2, "b_f")[0:HEADS, :], None, ALU.add).then_inc(f_asked, 1)
                        dve.wait_ge(f_logged, c.cum.at(1))
                        dve.scalar_tensor_tensor(f_row, f_row, 0.0, f_abs, ALU.min, ALU.subtract)
                        dve.drain()
                        dve.tensor_scalar(f_row, f_row, -1.0, None, ALU.mult)
                        dve.drain()
                        dve.tensor_tensor_scan(neg_cum_f, ones[0:HEADS, :], f_row, 0.0, ALU.mult, ALU.add).then_inc(cum_ready, 1)
                        c.cum.n += 1
                    if j:
                        recurrence(j - 1)
                    conv4(j)
                    pass_a(2)

                def beside_first(n):
                    if n == 3:
                        recurrence(3)

                queries_keys_values(0, beside_first)
                for m in range(0, KT, 2):
                    pass_a(2)
                    dve.wait_ge(act_evacuated, c.act.at(0))
                    gated(merged2, m, True)
                    gated(merged2, m + 1, True)
                for g in range(1, 4):
                    queries_keys_values(g, lambda n: attend(g - 1, n))
                for n in range(STEPS):
                    attend(3, n)
                    if n % 2 == 0:
                        pass_a()
                pass_a(KT - (STEPS + 1) // 2)
                dve.wait_ge(act_evacuated, c.act.at(0))
                for m in range(KT):
                    gated(merged2, m, False, attn_gate(m))
                split_merged(merged2)
                dve.drain()
                add_tiles([(m, 1.0) for m in range(KT)], True)
                dve.drain()
                norm(par(PAR2, "ffn2_g", 0, KT))
                ffn(False)
            assert c.dve.at(0) == V_TILES, c.dve.n


def kernel(**inputs):
    import numpy as np
    import concourse.bacc as bacc
    from concourse.bass_utils import run_bass_kernel_spmd as run

    a = {k: np.asarray(v) for k, v in inputs.items()}

    def tall(v):
        return np.ascontiguousarray(np.reshape(v, (-1, P)).T)

    def units(w):
        return w.reshape(KT, P, -1, P).transpose(2, 1, 0, 3).reshape(-1, P, D)

    def halves(w):
        return w.reshape(4, P, 4, 2 * P).transpose(2, 1, 0, 3).reshape(4, P, D)

    def moving(w):
        rows = D // w.shape[1]
        return w.reshape(KT // rows, rows, P, -1).transpose(0, 2, 1, 3).reshape(-1, P, D)

    def downs(w):
        return w.reshape(-1, 2, P, 2, 4 * P).transpose(0, 3, 2, 1, 4).reshape(-1, 2, P, D)

    def weave(*parts):
        n = len(parts[0][0]) // parts[0][1]
        return [u for i in range(n) for w, k in parts for u in w[i * k:i * k + k]]

    def chunks(ups, down):
        out = list(ups[0])
        for i in range(1, len(ups)):
            out += list(ups[i]) + list(down[i - 1])
        return out + list(down[-1])

    w = a["w_in"][0]
    cut = lambda at, n: w[:, at:at + n]
    w1, w2 = units(a["mlp_w1"][0]), downs(a["mlp_w2"][0])
    gate = units(cut(4608, 3 * D))
    order = weave((units(cut(0, 512)), 1), (units(cut(512, 512)), 1))
    order += list(units(cut(1024, 1024))) + list(moving(cut(2048, 512))) + list(units(cut(2560, 512)))
    sb_qk = weave((units(cut(3072, 512)), 1), (units(cut(3584, 512)), 1))
    conv_proj, hgrn_proj = halves(a["w_conv_proj"][0]), halves(a["w_hgrn_proj"][0])
    order += list(moving(cut(4096, 256))) + list(gate[0:2]) + sb_qk[0:2] + [conv_proj[0]] + sb_qk[2:4]
    for h in range(1, HG_HEADS):
        order += list(gate[2 * h:2 * h + 2]) + [conv_proj[h]] + (sb_qk[2 * h + 2:2 * h + 4] or list(moving(cut(4352, 256))))
    for g in range(4):
        order += list(gate[8 + 2 * g:10 + 2 * g]) + list(gate[16 + 2 * g:18 + 2 * g]) + [hgrn_proj[g]]
    order += list(halves(a["w_sb_proj"][0]))
    order += list(units(a["w_out"][0]))
    order += chunks([w1[2 * i:2 * i + 2] for i in range(MLP_CHUNKS)], w2)

    lru, par2 = [], []
    for l in range(LAYERS):
        def ffn(n):
            g, u = units(a[f"ffn{n}_w_gate_2"][l]), units(a[f"ffn{n}_w_up_2"][l])
            return chunks([list(g[2 * i:2 * i + 2]) + list(u[2 * i:2 * i + 2]) for i in range(FFN_CHUNKS)], downs(a[f"ffn{n}_w_down_2"][l]))

        w, b = a["w_in_2"][l], a["b_in_2"][l]
        at = 3 * D + HEADS
        order += ffn(1)
        recurrent = weave((units(cut(at, D)), 2), (units(cut(at + D, D)), 2))
        forget = np.concatenate([w[:, 3 * D:at], np.zeros((D, P - HEADS), np.float32)], axis=1)
        order += recurrent[0:2] + list(units(forget)) + recurrent[2:]
        qkv = [list(units(cut(2 * P * g, 2 * P))) + list(units(cut(D + 2 * P * g, 2 * P))) + list(moving(cut(2 * D + 2 * P * g, 2 * P)))
               for g in range(4)]
        order += qkv[0] + weave((units(cut(at + 3 * D, D)), 2), (units(a["w_o_rnn_2"][l]), 2)) + qkv[1] + qkv[2] + qkv[3]
        order += list(units(cut(at + 2 * D, D))) + list(units(a["w_o_attn_2"][l]))
        order += list(units(a["w_out_2"][l]))
        order += ffn(2)

        block = np.zeros((P, 2, KT, P), np.float32)
        for n, name in enumerate(("lru_w_a_2", "lru_w_x_2")):
            pairs = a[name][l].reshape(KT, 2, 64, 64)
            block[0:64, n, :, 0:64] = pairs[:, 0].transpose(1, 0, 2)
            block[64:128, n, :, 64:128] = pairs[:, 1].transpose(1, 0, 2)
        lru.append(block.reshape(P, -1))
        b_f = np.zeros((P, 1), np.float32)
        b_f[0:HEADS, 0] = b[3 * D:at]
        par2.append(np.concatenate([
            tall(a["ffn1_norm_2"][l]), tall(a["mix_norm_2"][l]), tall(a["ffn2_norm_2"][l]), tall(b[0:D]), tall(b[D:2 * D]),
            tall(b[2 * D:3 * D]), b_f, tall(b[at:at + D]), tall(b[at + D:at + 2 * D]), tall(b[at + 2 * D:at + 3 * D]),
            tall(b[at + 3 * D:at + 4 * D]), tall(a["q_norm_2"][l]), tall(a["k_norm_2"][l]), tall(a["conv_w_2"][l]),
            tall(a["conv_b_2"][l]), tall(a["lru_b_a_2"][l]), tall(a["lru_b_x_2"][l]), tall(a["lru_lambda_2"][l])], axis=1))
    assert len(order) == UNITS
    order += [np.zeros((P, D), np.float32)] * RING

    twice = lambda v: np.concatenate([v, v], axis=1)
    par1 = np.concatenate([
        tall(a["mod_b"]), tall(a["norm1_g"]), tall(a["gate_b"]), tall(a["conv_w"]), tall(a["conv_b"]), tall(a["conv_ln_g"]),
        tall(a["conv_ln_b"]), tall(a["hgrn_lb"]), tall(a["hgrn_norm_g"]), tall(twice(a["sb_qn_g"])), tall(twice(a["sb_kn_g"])),
        tall(a["norm2_g"])], axis=1)
    arrays = {
        "x_t": np.ascontiguousarray(a["x"][0].T.reshape(KT, P, S).transpose(1, 0, 2)),
        "c_row": np.ascontiguousarray(a["c"]),
        "par1": np.ascontiguousarray(par1),
        "par2": np.ascontiguousarray(np.stack(par2)),
        "lru": np.ascontiguousarray(np.stack(lru)),
        "mod_w": np.ascontiguousarray(a["mod_w"][0].T.reshape(MODS, P, D)),
        "stream": np.ascontiguousarray(np.stack(order)),
    }
    nc = bacc.Bacc("TRN2", target_bir_lowering=False, num_devices=1, dynamic_dma_scratch_size=1024)
    args = [nc.dram_tensor(f"in_{n}", v.shape, F32, kind="ExternalInput").ap() for n, v in arrays.items()]
    out = nc.dram_tensor("out_t", (P, KT, S), F32, kind="ExternalOutput").ap()
    build(nc, *args, out)
    r = run(nc, [{f"in_{n}": v for n, v in arrays.items()}], core_ids=[0])
    return np.ascontiguousarray(r.results[0]["out_t"].transpose(2, 1, 0).reshape(1, S, D))
```
